# Optimizing a Trainium2 kernel written in Bass

```python
import math
import numpy as np
import jax
import jax.numpy as jnp
from jax import lax
import jax, jax.numpy as jnp

D_MODEL = 1024
BATCH = 1
SEQ = 1024
DEPTH = 1

GRID_W = 64
CTX_LEN = 256

RWKV_WIDTH = 512
RWKV_HEAD = 64
RWKV_HEADS = RWKV_WIDTH // RWKV_HEAD
DECAY_LORA = 32
AAA_LORA = 32
GATE_LORA = 96
DIFF_WIDTH = D_MODEL - RWKV_WIDTH
DIFF_HEAD = 64
DIFF_HEADS = DIFF_WIDTH // (2 * DIFF_HEAD)
D_FF = 2816
CONV_W = 3
Q_BLOCK = 128
ROPE_THETA = 10000.0
NORM_EPS = 1e-6
LN_X_EPS = 64e-5
SUBLN_EPS = 1e-5
ATTN_SCALE = DIFF_HEAD ** -0.5

RWKV_SPLITS = (RWKV_WIDTH, 2 * RWKV_WIDTH, 3 * RWKV_WIDTH,
               3 * RWKV_WIDTH + DECAY_LORA, 3 * RWKV_WIDTH + DECAY_LORA + AAA_LORA)
RWKV_COLS = 3 * RWKV_WIDTH + DECAY_LORA + AAA_LORA + GATE_LORA
DIFF_QK = DIFF_HEADS * 2 * DIFF_HEAD
DIFF_V = DIFF_HEADS * 2 * DIFF_HEAD
IN_COLS = RWKV_COLS + 2 * DIFF_QK + DIFF_V


def rmsnorm(x, g, eps=NORM_EPS):
    xf = x.astype(jnp.float32)
    y = xf * lax.rsqrt(jnp.mean(xf * xf, axis=-1, keepdims=True) + eps)
    return (y * g.astype(jnp.float32)).astype(x.dtype)

def modulate(h, shift, scale):
    return h * (1.0 + scale) + shift

def adaln(cond, w_mod, b_mod):
    return jax.nn.silu(cond) @ w_mod + b_mod

def dwconv(x, w):
    return lax.conv_general_dilated(
        x, w[:, None, :].astype(x.dtype), window_strides=(1,),
        padding=((CONV_W // 2, CONV_W // 2),),
        dimension_numbers=('NWC', 'WIO', 'NWC'),
        feature_group_count=x.shape[-1])

def axial_rope(rows):
    n_pair = DIFF_HEAD // 4
    row = jnp.repeat(jnp.arange(rows, dtype=jnp.float32), GRID_W)
    col = jnp.tile(jnp.arange(GRID_W, dtype=jnp.float32), rows)
    inv = ROPE_THETA ** (-jnp.arange(n_pair, dtype=jnp.float32) / n_pair)
    ang = jnp.concatenate([row[:, None] * inv, col[:, None] * inv], axis=-1)
    return jnp.cos(ang), jnp.sin(ang)

def apply_rope(x, cos, sin):
    half = DIFF_HEAD // 2
    x1, x2 = x[..., :half], x[..., half:]
    return jnp.concatenate([x1 * cos - x2 * sin, x1 * sin + x2 * cos], axis=-1).astype(x.dtype)

def rwkv_prepare(rw, p):
    B, T, _ = rw.shape
    heads = lambda t: t.reshape(B, T, RWKV_HEADS, RWKV_HEAD)
    r, k, v, wl, al, gl = jnp.split(rw, RWKV_SPLITS, axis=-1)
    kk = heads(k * p['k_k']).astype(jnp.float32)
    kk = kk / jnp.maximum(jnp.linalg.norm(kk, axis=-1, keepdims=True), 1e-12)
    w_lat = jnp.tanh(wl)
    dirs = []
    for w0, w2, a0, a2 in ((p['w0_fwd'], p['w2_fwd'], p['a0_fwd'], p['a2_fwd']),
                           (p['w0_bwd'], p['w2_bwd'], p['a0_bwd'], p['a2_bwd'])):
        w = -jax.nn.softplus(-(w0 + w_lat @ w2).astype(jnp.float32)) - 0.5
        decay = jnp.exp(-jnp.exp(w))
        a = jax.nn.sigmoid((a0 + al @ a2).astype(jnp.float32))
        k_dir = k * (1.0 + (a - 1.0) * p['k_a'])
        dirs.append((heads(decay), heads(k_dir), heads(a)))
    return heads(r), heads(v), kk, gl, dirs

def rwkv_scan(r, decay, k, v, kk, a, s0, reverse):
    tm = lambda t: jnp.swapaxes(t, 0, 1)

    def step(S, inp):
        r_t, w_t, k_t, v_t, kk_t, b_t = inp
        sa = jnp.einsum('bhvk,bhk->bhv', S, kk_t)
        S = (S * w_t[:, :, None, :] - sa[..., None] * b_t[:, :, None, :]
             + v_t[..., None] * k_t[:, :, None, :])
        return S, jnp.einsum('bhvk,bhk->bhv', S, r_t)

    s_fin, ys = lax.scan(step, s0, (tm(r), tm(decay), tm(k), tm(v), tm(kk), tm(kk * a)),
                         reverse=reverse)
    return tm(ys), s_fin

def rwkv_output(y, r, v, k_bonus, gl, p):
    B, T = y.shape[:2]
    mu = jnp.mean(y, axis=-1, keepdims=True)
    var = jnp.mean(jnp.square(y - mu), axis=-1, keepdims=True)
    yn = ((y - mu) * lax.rsqrt(var + LN_X_EPS)).reshape(B, T, RWKV_WIDTH) * p['ln_x_w'] + p['ln_x_b']
    bonus = (jnp.sum(r * k_bonus * p['r_k'], axis=-1, keepdims=True) * v).reshape(B, T, RWKV_WIDTH)
    g = jax.nn.sigmoid(gl) @ p['g2']
    return ((yn + bonus) * g).astype(r.dtype)

def rwkv_mixer(rw, rw_c, p, need_ctx):
    r, v, kk, gl, dirs = rwkv_prepare(rw, p)
    r_c, v_c, kk_c, gl_c, dirs_c = rwkv_prepare(rw_c, p)
    s0 = jnp.zeros((rw.shape[0], RWKV_HEADS, RWKV_HEAD, RWKV_HEAD), jnp.float32)
    ys, ys_c = [], []
    for d, reverse in enumerate((False, True)):
        dec_c, k_c, a_c = dirs_c[d]
        yd_c, s_ctx = rwkv_scan(r_c, dec_c, k_c, v_c, kk_c, a_c, s0, reverse)
        dec, k_d, a_d = dirs[d]
        yd, _ = rwkv_scan(r, dec, k_d, v, kk, a_d, s_ctx, reverse)
        ys.append(yd)
        ys_c.append(yd_c)
    out = rwkv_output(ys[0] + ys[1], r, v, 0.5 * (dirs[0][1] + dirs[1][1]), gl, p)
    out_c = (rwkv_output(ys_c[0] + ys_c[1], r_c, v_c, 0.5 * (dirs_c[0][1] + dirs_c[1][1]), gl_c, p)
             if need_ctx else None)
    return out, out_c

def diff_split(dq):
    B, T, _ = dq.shape
    q, k, v = jnp.split(dq, (DIFF_QK, 2 * DIFF_QK), axis=-1)
    qk = lambda t: t.reshape(B, T, DIFF_HEADS, 2, DIFF_HEAD).transpose(0, 2, 3, 1, 4)
    return qk(q), qk(k), v.reshape(B, T, DIFF_HEADS, 2 * DIFF_HEAD).transpose(0, 2, 1, 3)

def diff_attention(q, k_all, v_all, lam):
    s = jnp.einsum('bhmqd,bhmkd->bhmqk', q, k_all).astype(jnp.float32) * ATTN_SCALE
    pr = jax.nn.softmax(s, axis=-1)
    a = pr[:, :, 0] - lam * pr[:, :, 1]
    return jnp.einsum('bhqk,bhke->bhqe', a.astype(v_all.dtype), v_all)

def diff_post(o, p, lam_init):
    B, H, T, e = o.shape
    o = rmsnorm(o, p['subln_w'], SUBLN_EPS) * (1.0 - lam_init)
    return o.transpose(0, 2, 1, 3).reshape(B, T, H * e)

def diff_mixer(dq, dq_c, p, lam_init, cos, sin, need_ctx):
    q, k, v = diff_split(dq)
    q_c, k_c, v_c = diff_split(dq_c)
    q, k = apply_rope(q, cos, sin), apply_rope(k, cos, sin)
    f32 = lambda t: t.astype(jnp.float32)
    lam = (jnp.exp(jnp.sum(f32(p['lam_q1']) * f32(p['lam_k1'])))
           - jnp.exp(jnp.sum(f32(p['lam_q2']) * f32(p['lam_k2']))) + lam_init)
    k_all = jnp.concatenate([k_c, k], axis=3)
    v_all = jnp.concatenate([v_c, v], axis=2)
    B, H, _, T, d = q.shape
    nb = T // Q_BLOCK
    qb = q.reshape(B, H, 2, nb, Q_BLOCK, d).transpose(3, 0, 1, 2, 4, 5)
    o = lax.map(lambda qq: diff_attention(qq, k_all, v_all, lam), qb)
    o = o.transpose(1, 2, 0, 3, 4).reshape(B, H, T, 2 * d)
    out = diff_post(o, p, lam_init)
    out_c = diff_post(diff_attention(q_c, k_c, v_c, lam), p, lam_init) if need_ctx else None
    return out, out_c

def token_mixer(h, h_c, p, lam_init, cos, sin, need_ctx):
    parts = h @ p['w_in']
    parts_c = h_c @ p['w_in']
    rw = dwconv(parts[..., :RWKV_COLS], p['rwkv_conv'])
    rw_c = dwconv(parts_c[..., :RWKV_COLS], p['rwkv_conv'])
    y_r, y_r_c = rwkv_mixer(rw, rw_c, p, need_ctx)
    y_d, y_d_c = diff_mixer(parts[..., RWKV_COLS:], parts_c[..., RWKV_COLS:], p, lam_init,
                            cos, sin, need_ctx)
    out = jnp.concatenate([y_r, y_d], axis=-1) @ p['w_out']
    out_c = jnp.concatenate([y_r_c, y_d_c], axis=-1) @ p['w_out'] if need_ctx else None
    return out, out_c

def conv_ffn(h, p):
    u = dwconv(h @ p['w_up'], p['ffn_conv']) + p['ffn_conv_b']
    val, gate = jnp.split(u, 2, axis=-1)
    return (val * jax.nn.silu(gate)) @ p['w_down']

def first_inputs(seed: int = 0) -> dict:
    key = jax.random.key(seed)
    keys = jax.random.split(key, 36)
    L, D, Rw = DEPTH, D_MODEL, RWKV_WIDTH

    def nrm(i, shape, s):
        return s * jax.random.normal(keys[i], shape, jnp.float32)

    def uni(i, shape, lo, hi):
        return jax.random.uniform(keys[i], shape, jnp.float32, lo, hi)

    conv_base = jnp.array([0.25, 0.5, 0.25], jnp.float32)[None, :, None]
    return {
        'x': nrm(0, (BATCH, SEQ, D), 1.0),
        'c': nrm(1, (BATCH, D), 1.0),
        'ctx': nrm(2, (BATCH, CTX_LEN, D), 1.0),
        'c_ctx': nrm(3, (D,), 1.0),
        'w_mod': nrm(4, (L, D, 6 * D), 0.5 * D ** -0.5),
        'b_mod': nrm(5, (L, 6 * D), 0.02),
        'g_pre_mix': 1.0 + nrm(6, (L, D), 0.05),
        'g_post_mix': 1.0 + nrm(7, (L, D), 0.05),
        'g_pre_ffn': 1.0 + nrm(8, (L, D), 0.05),
        'g_post_ffn': 1.0 + nrm(9, (L, D), 0.05),
        'w_in': nrm(10, (L, D, IN_COLS), D ** -0.5),
        'rwkv_conv': conv_base + nrm(11, (L, CONV_W, RWKV_COLS), 0.1),
        'w0_fwd': uni(12, (L, Rw), -6.5, -1.5),
        'w2_fwd': nrm(13, (L, DECAY_LORA, Rw), 0.1),
        'a0_fwd': nrm(14, (L, Rw), 0.1),
        'a2_fwd': nrm(15, (L, AAA_LORA, Rw), 0.1),
        'w0_bwd': uni(16, (L, Rw), -6.5, -1.5),
        'w2_bwd': nrm(17, (L, DECAY_LORA, Rw), 0.1),
        'a0_bwd': nrm(18, (L, Rw), 0.1),
        'a2_bwd': nrm(19, (L, AAA_LORA, Rw), 0.1),
        'g2': nrm(20, (L, GATE_LORA, Rw), GATE_LORA ** -0.5),
        'k_k': 0.85 + nrm(21, (L, Rw), 0.05),
        'k_a': 1.0 + nrm(22, (L, Rw), 0.05),
        'r_k': nrm(23, (L, RWKV_HEADS, RWKV_HEAD), 0.1),
        'ln_x_w': 1.0 + nrm(24, (L, Rw), 0.05),
        'ln_x_b': nrm(25, (L, Rw), 0.02),
        'lam_q1': nrm(26, (L, DIFF_HEAD), 0.1),
        'lam_k1': nrm(27, (L, DIFF_HEAD), 0.1),
        'lam_q2': nrm(28, (L, DIFF_HEAD), 0.1),
        'lam_k2': nrm(29, (L, DIFF_HEAD), 0.1),
        'subln_w': 1.0 + nrm(30, (L, 2 * DIFF_HEAD), 0.05),
        'w_out': nrm(31, (L, D, D), D ** -0.5),
        'w_up': nrm(32, (L, D, 2 * D_FF), D ** -0.5),
        'ffn_conv': conv_base + nrm(33, (L, CONV_W, 2 * D_FF), 0.1),
        'ffn_conv_b': nrm(34, (L, 2 * D_FF), 0.02),
        'w_down': nrm(35, (L, D_FF, D), D_FF ** -0.5),
    }

def first_block(x, c, ctx, c_ctx, w_mod, b_mod, g_pre_mix, g_post_mix, g_pre_ffn, g_post_ffn,
              w_in, rwkv_conv, w0_fwd, w2_fwd, a0_fwd, a2_fwd, w0_bwd, w2_bwd, a0_bwd, a2_bwd,
              g2, k_k, k_a, r_k, ln_x_w, ln_x_b, lam_q1, lam_k1, lam_q2, lam_k2, subln_w,
              w_out, w_up, ffn_conv, ffn_conv_b, w_down):
    n_tok = x.shape[1]
    ROWS = n_tok // GRID_W
    cos, sin = axial_rope(ROWS)
    for l in range(DEPTH):
        p = dict(g_pre_mix=g_pre_mix[l], g_post_mix=g_post_mix[l], g_pre_ffn=g_pre_ffn[l],
                 g_post_ffn=g_post_ffn[l], w_in=w_in[l], rwkv_conv=rwkv_conv[l],
                 w0_fwd=w0_fwd[l], w2_fwd=w2_fwd[l], a0_fwd=a0_fwd[l], a2_fwd=a2_fwd[l],
                 w0_bwd=w0_bwd[l], w2_bwd=w2_bwd[l], a0_bwd=a0_bwd[l], a2_bwd=a2_bwd[l],
                 g2=g2[l], k_k=k_k[l], k_a=k_a[l], r_k=r_k[l], ln_x_w=ln_x_w[l], ln_x_b=ln_x_b[l],
                 lam_q1=lam_q1[l], lam_k1=lam_k1[l], lam_q2=lam_q2[l], lam_k2=lam_k2[l],
                 subln_w=subln_w[l], w_out=w_out[l], w_up=w_up[l], ffn_conv=ffn_conv[l],
                 ffn_conv_b=ffn_conv_b[l], w_down=w_down[l])
        lam_init = 0.8 - 0.6 * math.exp(-0.3 * l)
        need_ctx = l + 1 < DEPTH
        mod = adaln(c, w_mod[l], b_mod[l])[:, None, :]
        mod_c = adaln(c_ctx[None, :], w_mod[l], b_mod[l])[:, None, :]
        sh1, sc1, gt1, sh2, sc2, gt2 = jnp.split(mod, 6, axis=-1)
        sh1c, sc1c, gt1c, sh2c, sc2c, gt2c = jnp.split(mod_c, 6, axis=-1)
        h = modulate(rmsnorm(x, p['g_pre_mix']), sh1, sc1)
        h_c = modulate(rmsnorm(ctx, p['g_pre_mix']), sh1c, sc1c)
        y, y_c = token_mixer(h, h_c, p, lam_init, cos, sin, need_ctx)
        x = x + gt1 * rmsnorm(y, p['g_post_mix'])
        h = modulate(rmsnorm(x, p['g_pre_ffn']), sh2, sc2)
        x = x + gt2 * rmsnorm(conv_ffn(h, p), p['g_post_ffn'])
        if need_ctx:
            ctx = ctx + gt1c * rmsnorm(y_c, p['g_post_mix'])
            h_c = modulate(rmsnorm(ctx, p['g_pre_ffn']), sh2c, sc2c)
            ctx = ctx + gt2c * rmsnorm(conv_ffn(h_c, p), p['g_post_ffn'])
    return x


N_META = 16
FOURIER_GROUPS = 4
FOURIER_GROUP_DIM = 128
FOURIER_WIDTH = FOURIER_GROUPS * FOURIER_GROUP_DIM
CONV_HEADS = 8
CONV_HEAD_DIM = 64
CONV_WIDTH = CONV_HEADS * CONV_HEAD_DIM
CONV_TAPS = 3
N_BRANCHES = 2
RMS_EPS = 1e-6
IN_COLS_2 = FOURIER_WIDTH + 3 * CONV_WIDTH + N_BRANCHES * D_MODEL


def rmsnorm_2(x, g):
    xf = x.astype(jnp.float32)
    var = jnp.mean(xf * xf, axis=-1, keepdims=True)
    return (xf * lax.rsqrt(var + RMS_EPS) * g.astype(jnp.float32)).astype(x.dtype)

def centred_dwconv(x, w, b):
    half = CONV_TAPS // 2
    L = x.shape[1]
    xp = jnp.pad(x, ((0, 0), (half, half), (0, 0)))
    y = b
    for k in range(CONV_TAPS):
        y = y + xp[:, k:k + L] * w[k]
    return y

def fourier_mix(u):
    bn, L, _ = u.shape
    ug = u.astype(jnp.float32).reshape(bn, L, FOURIER_GROUPS, FOURIER_GROUP_DIM)
    f = jnp.fft.fft2(ug, axes=(1, 3), norm="ortho").real
    return f.reshape(bn, L, FOURIER_WIDTH).astype(u.dtype)

def second_inputs(seed: int = 0) -> dict:
    key = jax.random.key(seed)
    ks = jax.random.split(key, 20)
    f32 = jnp.float32

    def normal(k, shape, fan_in):
        return jax.random.normal(k, shape, f32) * (fan_in ** -0.5)

    def gain(k, shape):
        return 1.0 + 0.02 * jax.random.normal(k, shape, f32)

    def bias(k, shape):
        return 0.01 * jax.random.normal(k, shape, f32)

    return {
        "x": jax.random.normal(ks[0], (BATCH, SEQ, D_MODEL), f32),
        "meta_tokens": jax.random.normal(ks[1], (N_META, D_MODEL), f32),
        "g_mix_pre": gain(ks[2], (DEPTH, D_MODEL)),
        "w_in": normal(ks[3], (DEPTH, D_MODEL, IN_COLS_2), D_MODEL),
        "b_gates": bias(ks[4], (DEPTH, N_BRANCHES * D_MODEL)),
        "w_fourier": normal(ks[5], (DEPTH, FOURIER_WIDTH, D_MODEL), FOURIER_WIDTH),
        "conv_w_mix": normal(ks[6], (DEPTH, CONV_TAPS, CONV_WIDTH), CONV_TAPS),
        "conv_b_mix": bias(ks[7], (DEPTH, CONV_WIDTH)),
        "w_conv_out": normal(ks[8], (DEPTH, CONV_WIDTH, D_MODEL), CONV_WIDTH),
        "w_out": normal(ks[9], (DEPTH, D_MODEL, D_MODEL), D_MODEL),
        "g_mix_post": gain(ks[10], (DEPTH, D_MODEL)),
        "g_ffn_pre": gain(ks[11], (DEPTH, D_MODEL)),
        "w_up": normal(ks[12], (DEPTH, D_MODEL, 2 * D_FF), D_MODEL),
        "conv_w_ffn": normal(ks[13], (DEPTH, CONV_TAPS, 2 * D_FF), CONV_TAPS),
        "conv_b_ffn": bias(ks[14], (DEPTH, 2 * D_FF)),
        "w_down": normal(ks[15], (DEPTH, D_FF, D_MODEL), D_FF),
        "g_ffn_post": gain(ks[16], (DEPTH, D_MODEL)),
    }

def second_block(x, meta_tokens, g_mix_pre, w_in, b_gates, w_fourier, conv_w_mix, conv_b_mix,
              w_conv_out, w_out, g_mix_post, g_ffn_pre, w_up, conv_w_ffn, conv_b_ffn,
              w_down, g_ffn_post):
    bn = x.shape[0]
    meta = jnp.broadcast_to(meta_tokens[None].astype(x.dtype), (bn, N_META, D_MODEL))
    h_res = jnp.concatenate([meta, x], axis=1)
    L = h_res.shape[1]

    splits = [FOURIER_WIDTH,
              FOURIER_WIDTH + CONV_WIDTH,
              FOURIER_WIDTH + 2 * CONV_WIDTH,
              FOURIER_WIDTH + 3 * CONV_WIDTH]

    for l in range(DEPTH):
        h = rmsnorm_2(h_res, g_mix_pre[l])
        proj = h @ w_in[l]
        u_a, c_g, b_g, v_b, gate_logits = jnp.split(proj, splits, axis=-1)

        y_a = fourier_mix(u_a) @ w_fourier[l]

        conv_in = c_g * v_b
        y_b = (b_g * centred_dwconv(conv_in, conv_w_mix[l], conv_b_mix[l])) @ w_conv_out[l]

        gates = jax.nn.sigmoid((gate_logits + b_gates[l]).reshape(bn, L, N_BRANCHES, D_MODEL))
        merged = gates[:, :, 0] * y_a + gates[:, :, 1] * y_b
        mix_out = merged @ w_out[l]
        h_res = h_res + rmsnorm_2(mix_out, g_mix_post[l])

        h2 = rmsnorm_2(h_res, g_ffn_pre[l])
        up = centred_dwconv(h2 @ w_up[l], conv_w_ffn[l], conv_b_ffn[l])
        a, v = jnp.split(up, 2, axis=-1)
        ffn_out = (jax.nn.gelu(a) * v) @ w_down[l]
        h_res = h_res + rmsnorm_2(ffn_out, g_ffn_post[l])

    return h_res[:, N_META:]


def setup_inputs(seed=0):
    out = dict(first_inputs(seed))
    for name, value in second_inputs(seed + 1).items():
        if name != "x":
            out[name + "_2"] = value
    return out


def reference(
    x, c, ctx, c_ctx, w_mod, b_mod, g_pre_mix, g_post_mix, g_pre_ffn, g_post_ffn, w_in,
    rwkv_conv, w0_fwd, w2_fwd, a0_fwd, a2_fwd, w0_bwd, w2_bwd, a0_bwd, a2_bwd, g2, k_k, k_a,
    r_k, ln_x_w, ln_x_b, lam_q1, lam_k1, lam_q2, lam_k2, subln_w, w_out, w_up, ffn_conv,
    ffn_conv_b, w_down, meta_tokens_2, g_mix_pre_2, w_in_2, b_gates_2, w_fourier_2,
    conv_w_mix_2, conv_b_mix_2, w_conv_out_2, w_out_2, g_mix_post_2, g_ffn_pre_2, w_up_2,
    conv_w_ffn_2, conv_b_ffn_2, w_down_2, g_ffn_post_2,
):
    x = first_block(
        x, c, ctx, c_ctx, w_mod, b_mod, g_pre_mix, g_post_mix, g_pre_ffn, g_post_ffn, w_in,
        rwkv_conv, w0_fwd, w2_fwd, a0_fwd, a2_fwd, w0_bwd, w2_bwd, a0_bwd, a2_bwd, g2, k_k, k_a,
        r_k, ln_x_w, ln_x_b, lam_q1, lam_k1, lam_q2, lam_k2, subln_w, w_out, w_up, ffn_conv,
        ffn_conv_b, w_down,
    )
    return second_block(
        x, meta_tokens_2, g_mix_pre_2, w_in_2, b_gates_2, w_fourier_2, conv_w_mix_2,
        conv_b_mix_2, w_conv_out_2, w_out_2, g_mix_post_2, g_ffn_pre_2, w_up_2, conv_w_ffn_2,
        conv_b_ffn_2, w_down_2, g_ffn_post_2,
    )


_drawn_inputs = setup_inputs


def setup_inputs(seed=0):
    import zlib

    import numpy as np

    out = dict(_drawn_inputs(seed))
    spreads = {}
    factors = {'w2_fwd': 5.618,
     'a0_fwd': 8.0,
     'w2_bwd': 6.193,
     'a0_bwd': 8.0,
     'ln_x_w': 11.568,
     'ln_x_b': 29.327,
     'lam_q2': 7.03,
     'subln_w': 8.343,
     'ffn_conv_b': 3.419,
     'b_gates_2': 8.0,
     'conv_b_mix_2': 8.0,
     'g_mix_post_2': 3.672,
     'g_ffn_pre_2': 3.297,
     'conv_b_ffn_2': 7.119,
     'g_ffn_post_2': 16.993,
     'r_k': 3.762,
     'lam_k1': 2.829}
    for name, (base, spread) in spreads.items():
        noise = np.random.default_rng([zlib.crc32(name.encode()), seed]).standard_normal(out[name].shape)
        drawn = base * np.exp(spread * noise) if base else spread * noise
        out[name] = jnp.asarray(drawn.astype(out[name].dtype))
    for name, factor in factors.items():
        out[name] = (out[name] * factor).astype(out[name].dtype)
    return out
```

```python
import math
from contextlib import ExitStack, contextmanager

import numpy as np

import concourse.bass as bass
from concourse import mybir

ALU = mybir.AluOpType
ACT = mybir.ActivationFunctionType
AX = mybir.AxisListType
F32 = mybir.dt.float32
F32R = mybir.dt.float32r

P = 128
D = 1024
KD = D // P
SEQ = 1024
CTX = 256
ALL = CTX + SEQ
META = 16
L2 = META + SEQ
PAD2 = 1044
PIECE2 = PAD2 // 3
FF = 2816
KF = FF // P
FF2_IN = SEQ + 2
RW = 512
PAIRS = RW // P
HEADS = 4
RWKV_COLS = 1696
CH = 64
NB = 4
BT = CH * NB
GRID_W = 64
KEYT = ALL // P
EM = math.exp(-0.5)


class Kit:

    def sem(self, name):
        s = self.nc.alloc_semaphore(name)
        self.taken.append(s)
        return s

    @contextmanager
    def stage(self, nc):
        with nc.Block() as block:
            yield block
        if self.taken:
            nc.clear_and_free_semaphores(self.taken)
            nc.all_engine_barrier()
        self.taken = []


def plan_params(ins):
    v = lambda a: a.rearrange("a (t p) -> (a t) p", p=P)
    rows = [("c", v(ins["c"]), 8), ("c_ctx", ins["c_ctx"].rearrange("(t p) -> t p", p=P), 8),
            ("b_mod", v(ins["b_mod"]), 48)]
    for n in ("g_pre_mix", "g_post_mix", "g_pre_ffn", "g_post_ffn"):
        rows.append((n, v(ins[n]), 8))
    for n in ("w0_fwd", "w0_bwd", "a0_fwd", "a0_bwd", "k_k", "k_a", "ln_x_w", "ln_x_b"):
        rows.append((n, v(ins[n]), 4))
    rows.append(("r_k", ins["r_k"].rearrange("a (t e) k -> (a t) (e k)", e=2), 4))
    rows.append(("subln_w", ins["subln_w"], 1))
    for tap in range(3):
        w = ins["rwkv_conv"][0, tap]
        rows.append((f"rwkv_conv{tap}", w[0:13 * P].rearrange("(t p) -> t p", p=P), 13))
        rows.append((f"rwkv_conv_last{tap}", w[1568:1696].rearrange("(t p) -> t p", p=P), 1))
    for tap in range(3):
        rows.append((f"ffn_conv{tap}", ins["ffn_conv"][0, tap].rearrange("(t p) -> t p", p=P), 2 * KF))
        rows.append((f"conv_w_ffn_2{tap}", ins["conv_w_ffn_2"][0, tap].rearrange("(t p) -> t p", p=P), 2 * KF))
        rows.append((f"conv_w_mix_2{tap}", ins["conv_w_mix_2"][0, tap].rearrange("(t p) -> t p", p=P), 4))
    rows.append(("ffn_conv_b", v(ins["ffn_conv_b"]), 2 * KF))
    rows.append(("conv_b_ffn_2", v(ins["conv_b_ffn_2"]), 2 * KF))
    rows.append(("conv_b_mix_2", v(ins["conv_b_mix_2"]), 4))
    rows.append(("b_gates_2", v(ins["b_gates_2"]), 16))
    for n in ("g_mix_pre_2", "g_mix_post_2", "g_ffn_pre_2", "g_ffn_post_2"):
        rows.append((n, v(ins[n]), 8))
    at, col, placed = 0, {}, []
    for name, src, n in rows:
        if at // P != (at + n - 1) // P:
            at = (at // P + 1) * P
        col[name] = at
        placed.append((name, src, n, at))
        at += n
    return placed, col, (at + P - 1) // P


def memory(nc, k):
    base = (nc.sbuf_base + 63) // 64 * 64
    k.top = 0

    def at(name, cols, offset, dt=F32, parts=P):
        n = int(np.prod(cols))
        k.top = max(k.top, offset + 4 * n)
        return nc.alloc_sbuf_tensor_at(name, [parts] + list(cols), dt, offset=base + offset)

    k.at = at
    k.limit = nc.sbuf_usable_end - base
    k.prm = at("prm", [k.n_batches * P], 0)
    small = k.n_batches * P * 4

    def keep(name, cols):
        nonlocal small
        t = at(name, cols, small)
        small += (4 * int(np.prod(cols)) + 31) // 32 * 32
        assert small <= 8192
        return t

    k.ident = keep("ident", [P])
    k.ones = keep("ones", [P])
    k.halves = keep("halves", [P])
    k.id64 = keep("id64", [CH])
    k.mod = keep("mod", [48, 2])
    k.scale = keep("scale", [8, KD])
    k.lam = keep("lam", [16])
    k.stat = keep("stat", [4, 16])
    k.silu_c = keep("silu_c", [KD, 2])
    k.w_raw = at("w_raw", [2, KD * P], 8192)
    k.w_hi = at("w_hi", [2, KD * P], 16384, F32R)
    k.w_lo = at("w_lo", [2, KD * P], 24576, F32R)
    k.xs = [at(f"xs{s}", [1296], 32768 + 5184 * s) for s in range(2)]
    FREE = 43136
    k.rbc = at("rbc", [ALL], FREE)
    k.sq = at("sq", [2, ALL], FREE + 5120)
    k.dg = at("dg", [10, P], FREE + 15360)
    k.BIG = FREE + 20480
    k.SPLIT = 133248


def rows_of(k, name, t=0):
    c = k.col[name] + t
    return k.prm[:, c:c + 1] if isinstance(c, int) else k.prm[:, bass.ds(c, 1)]


def split_tiles(eng, total, body, step=2):
    for n in range(step):
        body(n, 0, n)
    if total // step - 1 > 1:
        with eng.Fori(1, total // step - 1) as i:
            for r in range(step):
                body(i * step + r, i, r)
    if total > step:
        for n in range(total - step, total):
            body(n, n // step, n % step)


def setup_stage(nc, k):
    sem = k.sem
    rows_landed, const_ready = sem("rows_landed"), sem("const_ready")
    cols_ready, cols_out, c_ready = sem("cols_ready"), sem("cols_out"), sem("c_ready")
    ident_set = sem("ident_set")
    stage = k.at("param_rows", [k.n_batches, P], k.BIG)
    sig = k.at("sig_c", [KD, 2], k.BIG + 4096)
    ps = [k.psum[:, b, 0:P] for b in range(k.n_batches)]
    with k.stage(nc) as block:
        @block.sync
        def _(sp):
            sp.wait_ge(ident_set, 1)
            for name, src, n, at in k.placed:
                b, r = at // P, at % P
                sp.dma_start(stage[r:r + n, b, :], src).then_inc(rows_landed, 16)
            for dst, src in ((k.halves, k.ins["halves_k"]), (k.id64, k.ins["id64_k"])):
                sp.dma_start(dst[:, :], src).then_inc(rows_landed, 16)
            sp.wait_ge(rows_landed, 16 * (len(k.placed) + 2))

        @block.gpsimd
        def _(pool):
            nc.gpsimd.memset(stage[:, :, :], 0.0)
            nc.gpsimd.memset(k.ident[:, :], 0.0)
            pool.drain().then_inc(ident_set, 1)
            nc.gpsimd.affine_select(out=k.ident[:, :], in_=k.ident[:, :], compare_op=ALU.not_equal, fill=1.0,
                                    base=0, pattern=[[-1, P]], channel_multiplier=1).then_inc(const_ready, 1)

        @block.tensor
        def _(pe):
            pe.wait_ge(const_ready, 1)
            pe.wait_ge(rows_landed, 16 * (len(k.placed) + 2))
            for b in range(k.n_batches):
                nc.tensor.transpose(ps[b], stage[:, b, :], k.ident[:, :]).then_inc(cols_ready, 1)

        @block.vector
        def _(dve):
            nc.vector.memset(k.ones[:, :], 1.0)
            for s in range(2):
                nc.vector.memset(k.xs[s][:, :], 0.0)
            for b in range(k.n_batches):
                dve.wait_ge(cols_ready, b + 1)
                nc.vector.tensor_copy(k.prm[:, b * P:(b + 1) * P], ps[b]).then_inc(cols_out, 1)
            dve.wait_ge(c_ready, 1)
            for s, name in enumerate(("c", "c_ctx")):
                nc.vector.tensor_tensor(k.silu_c[:, :, s], k.prm[:, k.col[name]:k.col[name] + KD],
                                        sig[:, :, s], ALU.mult)

        @block.scalar
        def _(act):
            act.wait_ge(cols_out, k.n_batches)
            for s, name in enumerate(("c", "c_ctx")):
                last = nc.scalar.activation(sig[:, :, s], k.prm[:, k.col[name]:k.col[name] + KD], ACT.Sigmoid)
            act.drain().then_inc(c_ready, 1)


def adaln_stage(nc, k, name, t0, t1):
    sem = k.sem
    landed = [sem(f"{name}_landed{s}") for s in range(2)]
    summed, kept = sem(f"{name}_summed"), sem(f"{name}_kept")
    wbuf = k.at(f"{name}_w", [2, KD, 4 * P], k.SPLIT)
    groups = (t1 - t0) // 4
    src = k.ins["w_mod"][0].rearrange("(k p) n -> p k n", p=P)
    with k.stage(nc) as block:
        @block.sync
        def _(sp):
            def body(n, m, s):
                if not (isinstance(n, int) and n < 2):
                    sp.wait_ge(summed, n - 1)
                sp.dma_start(wbuf[:, s], src[:, :, bass.ds((n * 4 + t0) * P, 4 * P)]).then_inc(landed[s], 16)
            split_tiles(sp, groups, body)

        @block.tensor
        def _(pe):
            def body(n, m, s):
                pe.wait_ge(landed[s], m * 16 + 16)
                if not (isinstance(n, int) and n < 2):
                    pe.wait_ge(kept, n - 1)
                for j in range(4):
                    for kk in range(KD):
                        last = nc.tensor.matmul(k.psum[:, s, 2 * j:2 * j + 2], wbuf[:, s, kk, j * P:(j + 1) * P],
                                                k.silu_c[:, kk, :], start=(kk == 0), stop=(kk == KD - 1))
                last.then_inc(summed, 1)
            split_tiles(pe, groups, body)

        @block.vector
        def _(dve):
            def body(n, m, s):
                dve.wait_ge(summed, n + 1)
                for e in range(2):
                    last = nc.vector.tensor_tensor(
                        k.mod[:, bass.ds(n * 4 + t0, 4), e],
                        k.psum[:, s, e:e + 8:2],
                        k.prm[:, bass.ds(n * 4 + t0 + k.col["b_mod"], 4)], ALU.add)
                last.then_inc(kept, 1)
            split_tiles(dve, groups, body)


def load_turned(nc, k, name, srcs, dst):
    sem = k.sem
    landed = [sem(f"{name}_landed{s}") for s in range(2)]
    turned = sem(f"{name}_turned")
    kept = [sem(f"{name}_kept_by_vector"), sem(f"{name}_kept_by_scalar")]
    rows = [k.at(f"{name}_rows{s}", [D], k.SPLIT + 4096 * s) for s in range(2)]
    tiles = [(src, n, at, r) for src, tokens, at in srcs for r in range(0, tokens, P)
             for n in [min(P, tokens - r)]]
    with k.stage(nc) as block:
        @block.sync
        def _(sp):
            for n, (src, m, at, r) in enumerate(tiles):
                if n >= 2:
                    sp.wait_ge(turned, n - 1)
                sp.dma_start(rows[n % 2][0:m, :], src[r:r + m, :]).then_inc(landed[n % 2], 16)

        @block.tensor
        def _(pe):
            for n, (src, m, at, r) in enumerate(tiles):
                pe.wait_ge(landed[n % 2], 16 * (n // 2 + 1))
                if n >= 2:
                    for half in kept:
                        pe.wait_ge(half, n - 1)
                for kk in range(KD):
                    last = nc.tensor.transpose(k.psum[:, 2 * (n % 2) + kk // 4, (kk % 4) * P:(kk % 4) * P + m],
                                               rows[n % 2][0:m, kk * P:(kk + 1) * P], k.ident[0:m, 0:m])
                last.then_inc(turned, 1)

        def halves(half):
            for n, (src, m, at, r) in enumerate(tiles):
                out = dst[:, 4 * half:4 * half + 4, at + r:at + r + m]
                src_ps = k.psum[:, 2 * (n % 2) + half, :].rearrange("p (a b) -> p a b", a=4)[:, :, 0:m]
                yield n, out, src_ps

        @block.vector
        def _(dve):
            for n, out, src_ps in halves(0):
                dve.wait_ge(turned, n + 1)
                nc.vector.tensor_copy(out, src_ps).then_inc(kept[0], 1)

        @block.scalar
        def _(act):
            for n, out, src_ps in halves(1):
                act.wait_ge(turned, n + 1)
                nc.scalar.activation(out, src_ps, ACT.Copy).then_inc(kept[1], 1)


def token_scale(nc, k, name, src, N, eps):
    sem = k.sem
    squared, added = sem(f"{name}_squared"), sem(f"{name}_added")
    meaned, rooted, diags = sem(f"{name}_meaned"), sem(f"{name}_rooted"), sem(f"{name}_diags")
    spread = sem(f"{name}_spread")
    nt = (N + P - 1) // P
    size = [min(P, N - t * P) for t in range(nt)]
    tail = size[-1]
    st = k.psum[:, 0, 0:nt]
    with k.stage(nc) as block:
        @block.scalar
        def _(act):
            for kk in range(KD):
                if kk >= 2:
                    act.wait_ge(added, kk - 1)
                nc.scalar.activation(k.sq[:, kk % 2, 0:N], src(kk), ACT.Square).then_inc(squared, 1)
            act.wait_ge(meaned, 1)
            nc.scalar.activation(k.stat[:, 1, 0:nt], k.stat[:, 0, 0:nt], ACT.Sqrt).then_inc(rooted, 1)
            for j in range(0, nt, 4):
                act.wait_ge(spread, j // 4 + 1)
                m = min(N, (j + 4) * P) - j * P
                nc.scalar.activation(k.rbc[:, j * P:j * P + m], k.psum[:, 1 + j // 4, 0:m], ACT.Copy)

        @block.tensor
        def _(pe):
            for kk in range(KD):
                pe.wait_ge(squared, kk + 1)
                for t in range(nt):
                    last = nc.tensor.matmul(st[0:size[t], t:t + 1], k.sq[:, kk % 2, t * P:t * P + size[t]],
                                            k.ones[:, 0:1], start=(kk == 0 and t == 0), stop=(kk == KD - 1),
                                            skip_group_check=True)
                last.then_inc(added, 1)
            pe.wait_ge(diags, 1)
            for j in range(0, nt, 4):
                full = [t for t in range(j, min(nt, j + 4)) if size[t] == P]
                if full:
                    last = nc.tensor.matmul(k.psum[:, 1 + j // 4, 0:len(full) * P], k.ones[:, :],
                                            k.dg[:, j:j + len(full), :], start=True, stop=True)
                if j + 4 >= nt and tail < P:
                    o = (nt - 1 - j) * P
                    last = nc.tensor.matmul(k.psum[:, 1 + j // 4, o:o + tail], k.ones[0:tail, :],
                                            k.dg[0:tail, nt - 1, 0:tail], start=True, stop=True)
                last.then_inc(spread, 1)

        @block.vector
        def _(dve):
            nc.vector.memset(k.stat[:, 0, 0:nt], 1.0)
            dve.drain()
            dve.wait_ge(added, KD)
            for t0, t1, m in ((0, nt - 1, P), (nt - 1, nt, tail)):
                nc.vector.tensor_scalar(k.stat[0:m, 0, t0:t1], st[0:m, t0:t1], 1.0 / D, eps, ALU.mult, ALU.add)
            dve.drain().then_inc(meaned, 1)
            dve.wait_ge(rooted, 1)
            nc.vector.reciprocal(k.stat[:, 2, 0:nt], k.stat[:, 1, 0:nt])
            dve.drain()
            for t in range(nt):
                nc.vector.tensor_scalar(k.dg[:, t, :], k.ident[:, :], k.stat[:, 2, t:t + 1], None, ALU.mult)
            dve.drain().then_inc(diags, 1)


def modulate_split(nc, k, name, tiles, hi, lo):
    sem = k.sem
    scaled, shifted, high = sem(f"{name}_scaled"), sem(f"{name}_shifted"), sem(f"{name}_high")
    done = sem(f"{name}_low")
    with k.stage(nc) as block:
        @block.vector
        def _(dve):
            for n in range(len(tiles) + 1):
                if n < len(tiles):
                    kk, src, rc, oc, gain, shift = tiles[n]
                    m = rc.stop - rc.start
                    if n >= 2:
                        dve.wait_ge(high, n - 1)
                    nc.vector.tensor_tensor(k.sq[:, n % 2, 0:m], src, k.rbc[:, rc], ALU.mult).then_inc(scaled, 1)
                if n >= 1:
                    kk, src, rc, oc, gain, shift = tiles[n - 1]
                    m = rc.stop - rc.start
                    dve.wait_ge(high, n)
                    nc.vector.tensor_tensor(lo[:, kk, oc], k.xs[(n - 1) % 2][:, 4:4 + m],
                                            hi[:, kk, oc].bitcast(F32), ALU.subtract).then_inc(done, 1)

        @block.scalar
        def _(act):
            for n, (kk, src, rc, oc, gain, shift) in enumerate(tiles):
                m = rc.stop - rc.start
                act.wait_ge(scaled, n + 1)
                if n >= 2:
                    act.wait_ge(done, n - 1)
                nc.scalar.activation(k.xs[n % 2][:, 4:4 + m], k.sq[:, n % 2, 0:m], ACT.Identity,
                                     bias=shift, scale=gain).then_inc(shifted, 1)
                act.wait_ge(shifted, n + 1)
                nc.scalar.activation(hi[:, kk, oc], k.xs[n % 2][:, 4:4 + m], ACT.Copy).then_inc(high, 1)


def gains(nc, k, name, jobs):
    with k.stage(nc) as block:
        @block.vector
        def _(dve):
            for out, a, b, one in jobs:
                nc.vector.scalar_tensor_tensor(out=out, in0=b, scalar=1.0 if one else 0.0, in1=a,
                                               op0=ALU.add, op1=ALU.mult)


def project(nc, k, name, K, hi, lo, pieces, total, weight, act_evac, dve_evac=None, store=None,
            pair_index=False, quads=None):
    sem = k.sem
    w_landed = [sem(f"{name}_w_landed{s}") for s in range(2)]
    w_high, w_low = sem(f"{name}_w_high"), sem(f"{name}_w_low")
    acc_done, acc_read = sem(f"{name}_acc_done"), sem(f"{name}_acc_read")
    worked = sem(f"{name}_worked") if dve_evac else acc_read
    stored = [sem(f"{name}_stored{s}") for s in range(2)]
    past = lambda n, least: not (isinstance(n, int) and n < least)
    step = 4 if quads else 2
    passed = sem(f"{name}_passed") if quads else None
    acts = quads or [(K, hi, lo)] * 2
    tuples = pair_index or quads
    raw = [k.w_raw[:, r % 2, 0:acts[r][0] * P].rearrange("p (k n) -> p k n", n=P) for r in range(step)]
    w_hi = [k.w_hi[:, s, :].rearrange("p (k n) -> p k n", n=P) for s in range(2)]
    w_lo = [k.w_lo[:, s, :].rearrange("p (k n) -> p k n", n=P) for s in range(2)]

    def hold_sp(sp, s, value):
        sp.wait_ge(s, value)
        if quads:
            sp.sem_inc(passed, 1)

    with k.stage(nc) as block:
        @block.sync
        def _(sp):
            def body(n, i, r):
                if past(n, 2):
                    hold_sp(sp, w_low, n - 1)
                sp.dma_start(raw[r], weight(n if isinstance(n, int) or not tuples else (i, r))).then_inc(w_landed[r % 2], 16)
                if quads and store and r == 0 and past(n, 1):
                    hold_sp(sp, worked, n)
                    store(sp, i - 1).then_inc(stored[0], 16)
                elif store and not quads and past(n, 1):
                    sp.wait_ge(worked, n)
                    store(sp, n - 1, 1 - r).then_inc(stored[1 - r], 16)
            split_tiles(sp, total, body, step)
            if store:
                sp.wait_ge(worked, total)
                if quads:
                    store(sp, total // 4 - 1).then_inc(stored[0], 16)
                    sp.wait_ge(stored[0], 16 * (total // 4))
                else:
                    store(sp, total - 1, 1).then_inc(stored[1], 16)
                    for s in range(2):
                        sp.wait_ge(stored[s], 16 * (total // 2))

        @block.tensor
        def _(pe):
            def body(n, i, r):
                s = r % 2
                kt, xh, xl = acts[r]
                pe.wait_ge(w_low, n + 1)
                if past(n, 2):
                    pe.wait_ge(acc_read, n - 1)
                for j, (c0, cn) in enumerate(pieces):
                    out = k.psum[:, 3 * s + j, 0:cn]
                    for kk in range(kt):
                        for q, (w, x) in enumerate(((w_hi, xh), (w_lo, xh), (w_hi, xl))):
                            last = nc.tensor.matmul(out, w[s][:, kk, :], x[:, kk, c0:c0 + cn],
                                                    start=(kk == 0 and q == 0), stop=(kk == kt - 1 and q == 2))
                last.then_inc(acc_done, 1)
            split_tiles(pe, total, body, step)

        @block.scalar
        def _(act):
            def high(n, i, r):
                s, w = r % 2, acts[r][0] * P
                act.wait_ge(w_landed[s], i * (8 * step) + (r // 2) * 16 + 16)
                if past(n, 2):
                    act.wait_ge(acc_done, n - 1)
                nc.scalar.activation(k.w_hi[:, s, 0:w], k.w_raw[:, s, 0:w], ACT.Copy).then_inc(w_high, 1)

            def body(n, i, r):
                s = r % 2
                if not (isinstance(n, int) and n == total - 1):
                    high(n + 1, i + (r + 1) // step, (r + 1) % step)
                act.wait_ge(acc_done, n + 1)
                if past(n, 2):
                    if dve_evac:
                        act.wait_ge(worked, n - 1)
                    elif store:
                        act.wait_ge(stored[s], i * 16)
                act_evac(act, n, i, r, acc_read, worked)
            high(0, 0, 0)
            split_tiles(act, total, body, step)

        @block.vector
        def _(dve):
            def low(n, r):
                s, w = r % 2, acts[r][0] * P
                dve.wait_ge(w_high, n + 1)
                nc.vector.tensor_tensor(k.w_lo[:, s, 0:w], k.w_raw[:, s, 0:w],
                                        k.w_hi[:, s, 0:w].bitcast(F32), ALU.subtract).then_inc(w_low, 1)

            def body(n, i, r):
                if not (isinstance(n, int) and n == total - 1):
                    low(n + 1, (r + 1) % step)
                if dve_evac:
                    dve.drain()
                    dve.wait_ge(acc_read, n + 1)
                    if store and not quads and past(n, 2):
                        dve.wait_ge(stored[r], i * 16)
                    if store and quads and r == 2 and past(n, 4):
                        dve.wait_ge(stored[0], i * 16)
                    dve_evac(dve, n, i, r).then_inc(worked, 1)
            low(0, 0)
            split_tiles(dve, total, body, step)


def acc(k, s, n):
    return k.psum[:, 3 * s:3 * s + 3, :].rearrange("p a b -> p (a b)")[:, 0:n]


def in_projection(nc, k):
    w_in = k.ins["w_in"][0].rearrange("(k p) n -> p k n", p=P)
    pieces = [(0, 512), (512, 512), (1024, 256)]
    u = [k.at(f"conv_out{s}", [ALL], k.BIG + 5120 * s) for s in range(2)]
    first = [True]

    def rw_weight(n):
        return w_in[:, :, 1568:1696] if isinstance(n, int) and n == 13 else w_in[:, :, bass.ds(n * P, P)]

    def rw_act(act, n, m, s, acc_read, worked):
        nc.scalar.activation(k.xs[s][:, 1:1 + CTX], acc(k, s, CTX), ACT.Copy)
        nc.scalar.activation(k.xs[s][:, 2 + CTX:2 + ALL], acc(k, s, ALL)[:, CTX:ALL], ACT.Copy).then_inc(acc_read, 1)

    def rw_dve(dve, n, m, s):
        tap = [rows_of(k, f"rwkv_conv_last{j}" if isinstance(n, int) and n == 13 else f"rwkv_conv{j}",
                       0 if isinstance(n, int) and n == 13 else n) for j in range(3)]
        segments = ((0, CTX, 0), (CTX, SEQ, CTX + 1))
        for c, m, x in segments:
            nc.vector.tensor_scalar(u[s][:, c:c + m], k.xs[s][:, x + 1:x + 1 + m], tap[1], None, ALU.mult)
        for j in (0, 2):
            dve.drain()
            for c, m, x in segments:
                last = nc.vector.scalar_tensor_tensor(out=u[s][:, c:c + m], in0=k.xs[s][:, x + j:x + j + m],
                                                      scalar=tap[j], in1=u[s][:, c:c + m],
                                                      op0=ALU.mult, op1=ALU.add)
        return last

    clear_pads(nc, k, (0, 1 + CTX, 2 + ALL))
    project(nc, k, "rw", KD, k.h_hi, k.h_lo, pieces, 14, rw_weight, rw_act, rw_dve,
            store=lambda sp, n, s: sp.dma_start(at_tile(k.rw_dram, n), u[s][:, :]))

    def qkv_act(act, n, m, s, acc_read, worked):
        nc.scalar.activation(k.xs[s][:, 0:ALL], acc(k, s, ALL), ACT.Copy).then_inc(acc_read, 1)

    project(nc, k, "qkv", KD, k.h_hi, k.h_lo, pieces, 12,
            lambda n: w_in[:, :, bass.ds(n * P + RWKV_COLS, P)], qkv_act,
            store=lambda sp, n, s: sp.dma_start(at_tile(k.qkv_dram, n), k.xs[s][:, 0:ALL]))


def at_tile(dram, n):
    return dram[n] if isinstance(n, int) else dram[bass.ds(n, 1), :, :].rearrange("a p n -> (a p) n")


def clear_pads(nc, k, cols):
    with k.stage(nc) as block:
        @block.vector
        def _(dve):
            for s in range(2):
                for c in cols:
                    nc.vector.memset(k.xs[s][:, c:c + 1], 0.0)


def first_block(nc, k):
    ins = k.ins
    k.xT = k.at("x_t", [KD, ALL], k.BIG)
    setup_stage(nc, k)
    adaln_stage(nc, k, "mod1", 0, 16)
    load_turned(nc, k, "x", [(ins["ctx"][0], CTX, 0), (ins["x"][0], SEQ, CTX)], k.xT)
    save(nc, k, "x_save", k.x_dram, k.xT[:, :, CTX:ALL])
    k.h_hi = k.at("h1_hi", [KD, ALL], 104576 + 0, F32R)
    k.h_lo = k.at("h1_lo", [KD, ALL], 104576 + KD * ALL * 4, F32R)
    assert k.top <= k.limit, (k.top, k.limit)
    token_scale(nc, k, "pre1", lambda kk: k.xT[:, kk, :], ALL, 1e-6)
    col = lambda n: k.prm[:, k.col[n]:k.col[n] + KD]
    gains(nc, k, "g1", [(k.scale[:, s, :], col("g_pre_mix"), k.mod[:, 8:16, s], True) for s in range(2)])
    tiles = []
    for kk in range(KD):
        tiles.append((kk, k.xT[:, kk, 0:CTX], slice(0, CTX), slice(0, CTX),
                      k.scale[:, 1, kk:kk + 1], k.mod[:, kk, 1:2]))
        tiles.append((kk, k.xT[:, kk, CTX:ALL], slice(CTX, ALL), slice(CTX, ALL),
                      k.scale[:, 0, kk:kk + 1], k.mod[:, kk, 0:1]))
    modulate_split(nc, k, "h1", tiles, k.h_hi, k.h_lo)
    in_projection(nc, k)


def save(nc, k, name, dram, src):
    done = k.sem(f"{name}_done")
    with k.stage(nc) as block:
        @block.sync
        def _(sp):
            sp.dma_start(dram.rearrange("k p n -> p k n"), src).then_inc(done, 16)
            sp.wait_ge(done, 16)


class Direction:

    def __init__(self, qr, kb, vs, m1, atl, a_t, tt, x, z, w1, vu, kbs, yg, h):
        self.qr, self.kb, self.vs = qr, kb, vs
        self.m1, self.a_t, self.atl = m1, a_t, atl
        self.tt, self.x = tt, x
        self.z, self.w1 = z, w1
        self.vu, self.kbs = vu, kbs
        self.yg, self.h = yg, h


def rwkv_memory(nc, k):
    o = [8192]

    def at(name, cols, dt=F32):
        t = k.at(name, cols, o[0], dt)
        o[0] += (4 * int(np.prod(cols)) + 31) // 32 * 32
        return t

    k.ym = k.at("mixed", [KD, SEQ], 180032)
    k.lora_w = at("lora_w", [2, RW])
    k.g2_w = at("g2_w", [RW])
    k.omk = at("one_minus_k_a", [PAIRS])
    k.mask = [at(f"mask{d}", [2, P]) for d in range(2)]
    k.maskl = [at(f"mask_levels{d}", [6, CH]) for d in range(2)]
    k.sign = at("sign", [2, CH])
    k.lora = at("lora_in", [2, ALL])
    k.r, k.kx, k.v, k.kk = (at(n, [ALL]) for n in ("r_in", "k_in", "v_in", "kk"))
    k.tmp = at("tmp", [ALL])
    k.keep = at("keep", [ALL])
    k.pd = [[at(f"{n}{d}", [ALL]) for n in ("decay", "decay_before", "growth", "k_dir", "b")] for d in range(2)]
    k.yf = [at(f"y_dir{d}", [SEQ]) for d in range(2)]

    def half(d):
        cols = dict(qr=[NB, 2, CH], kb=[NB, 2, CH], vs=[NB, CH], m1=[NB, 2, P], atl=[6, NB, CH], a_t=[NB, CH],
                    tt=[2, NB, CH], x=[NB, CH], z=[NB, P], w1=[NB, CH], vu=[NB, 2, CH], kbs=[NB, 2, CH],
                    yg=[2, NB, CH], h=[NB, CH])
        return Direction(**{n: at(f"{n}_{d}", c) for n, c in cols.items()})
    k.dir = [half(d) for d in range(2)]
    assert o[0] <= 180032, o[0]


STEPS = ("staged", "v_staged", "products", "kb_kept", "masked", "turned", "levels", "started", "t_ready", "akv_kept",
         "x_done", "x_kept", "update_done", "updated", "w_done", "w_kept", "g_done", "g_kept",
         "h_done", "h_kept", "y_done", "y_kept")


def rwkv_setup(nc, k):
    sem = k.sem
    landed, cleared = sem("rw_const_landed"), sem("rw_const_cleared")
    ins = k.ins
    with k.stage(nc) as block:
        @block.sync
        def _(sp):
            sp.wait_ge(cleared, 1)
            pairs = [(k.sign, ins["sign_k"]), (k.lora[:, 0, :], k.rw_dram[12]), (k.lora[:, 1, :], k.rw_dram[13]),
                     (k.g2_w[32:128, :], ins["g2"][0])]
            for d, n in enumerate(("fwd", "bwd")):
                pairs += [(k.mask[d], ins["mask_k"][d]), (k.maskl[d], ins["levels_k"][d]),
                          (k.lora_w[0:32, d, :], ins[f"w2_{n}"][0]), (k.lora_w[32:64, d, :], ins[f"a2_{n}"][0])]
            for dst, src in pairs:
                sp.dma_start(dst if isinstance(dst, bass.AP) else dst[:], src).then_inc(landed, 16)
            sp.wait_ge(landed, 16 * len(pairs))

        @block.vector
        def _(dve):
            nc.vector.memset(k.g2_w[0:32, :], 0.0)
            nc.vector.memset(k.keep[:, :], 1.0)
            dve.drain().then_inc(cleared, 1)
            nc.vector.memset(k.keep[:, 0:ALL:CH], 0.0)
            c = k.col["k_a"]
            nc.vector.tensor_scalar(k.omk[:, :], k.prm[:, c:c + PAIRS], -1.0, 1.0, ALU.mult, ALU.add)

        @block.scalar
        def _(act):
            act.wait_ge(landed, 16 * 12)
            nc.scalar.activation(k.lora[0:32, 0, :], k.lora[0:32, 0, :], ACT.Tanh)
            nc.scalar.activation(k.lora[:, 1, :], k.lora[:, 1, :], ACT.Sigmoid)


def rwkv_prepare(nc, k, p):
    sem = k.sem
    landed = sem(f"prep{p}_landed")
    sq, sums, root, unit = (sem(f"prep{p}_{n}") for n in ("squared", "sums", "rooted", "scaled"))
    zs, za, gates, cum = (sem(f"prep{p}_{n}") for n in ("z", "za", "gates", "cumulated"))
    ps = [k.psum[:, 3 * s:3 * s + 3, :].rearrange("p a b -> p (a b)") for s in range(2)]
    pieces = [(0, 512), (512, 512), (1024, 256)]
    prm = lambda n: rows_of(k, n, p)
    with k.stage(nc) as block:
        @block.sync
        def _(sp):
            for dst, n in ((k.kx, 4 + p), (k.r, p), (k.v, 8 + p)):
                sp.dma_start(dst[:, :], k.rw_dram[n]).then_inc(landed, 16)
            sp.wait_ge(landed, 48)

        @block.tensor
        def _(pe):
            def spread(out, lhs, rhs):
                for c, m in pieces:
                    last = nc.tensor.matmul(out[:, c:c + m], lhs, rhs[:, c:c + m], start=True, stop=True)
                return last
            for d in range(2):
                if d == 1:
                    pe.wait_ge(gates, 1)
                spread(ps[0], k.lora_w[0:32, d, p * P:(p + 1) * P], k.lora[0:32, 0, :]).then_inc(zs, 1)
                if d == 1:
                    pe.wait_ge(gates, 2)
                spread(ps[1], k.lora_w[32:64, d, p * P:(p + 1) * P], k.lora[32:64, 0, :]).then_inc(za, 1)
            pe.wait_ge(gates, 3)
            pe.wait_ge(sq, 1)
            spread(ps[0], k.halves[:, :], k.tmp).then_inc(sums, 1)

        @block.scalar
        def _(act):
            for d, n in enumerate(("fwd", "bwd")):
                act.wait_ge(zs, d + 1)
                nc.scalar.activation(k.pd[d][1][:, :], ps[0][:, 0:ALL], ACT.Sigmoid, bias=prm(f"w0_{n}")).then_inc(gates, 1)
                act.wait_ge(za, d + 1)
                nc.scalar.activation(k.pd[d][4][:, :], ps[1][:, 0:ALL], ACT.Sigmoid, bias=prm(f"a0_{n}")).then_inc(gates, 1)
            act.wait_ge(sums, 1)
            nc.scalar.activation(k.tmp[:, :], ps[0][:, 0:ALL], ACT.Sqrt).then_inc(root, 1)
            for d in range(2):
                act.wait_ge(cum, d + 1)
                nc.scalar.activation(k.pd[d][2][:, :], k.pd[d][0][:, :], ACT.Exp, scale=EM)
                nc.scalar.activation(k.pd[d][1][:, :], k.pd[d][1][:, :], ACT.Exp, scale=-EM)
                act.drain()
                nc.scalar.activation(k.pd[d][0][:, :], k.pd[d][0][:, :], ACT.Exp, scale=-EM)

        @block.vector
        def _(dve):
            dve.wait_ge(landed, 48)
            nc.vector.tensor_scalar(k.kk[:, :], k.kx[:, :], prm("k_k"), None, ALU.mult)
            dve.drain()
            nc.vector.tensor_tensor(k.tmp[:, :], k.kk[:, :], k.kk[:, :], ALU.mult).then_inc(sq, 1)
            for d in range(2):
                dve.wait_ge(gates, 2 * d + 1)
                f = slice(None) if d == 0 else slice(None, None, -1)
                nc.vector.tensor_tensor_scan(k.pd[d][0][:, f], k.keep[:, :], k.pd[d][1][:, f], 0.0,
                                             ALU.mult, ALU.add)
                dve.drain()
                nc.vector.tensor_tensor(k.pd[d][1][:, :], k.pd[d][0][:, :], k.pd[d][1][:, :], ALU.subtract).then_inc(cum, 1)
                dve.wait_ge(gates, 2 * d + 2)
                nc.vector.tensor_scalar(k.pd[d][3][:, :], k.pd[d][4][:, :], prm("k_a"), k.omk[:, p:p + 1],
                                        ALU.mult, ALU.add)
                dve.drain()
                nc.vector.tensor_tensor(k.pd[d][3][:, :], k.pd[d][3][:, :], k.kx[:, :], ALU.mult)
            dve.wait_ge(root, 1)
            nc.vector.tensor_scalar(k.tmp[:, :], k.tmp[:, :], 1e-12, None, ALU.max)
            dve.drain()
            nc.vector.reciprocal(k.tmp[:, :], k.tmp[:, :])
            dve.drain()
            nc.vector.tensor_tensor(k.kk[:, :], k.kk[:, :], k.tmp[:, :], ALU.mult)
            dve.drain()
            for d in range(2):
                first, second = k.pd[d][3], k.pd[d][4]
                nc.vector.tensor_tensor(second[0:64, :], second[0:64, :], k.kk[0:64, :], ALU.mult)
                nc.vector.tensor_tensor(k.tmp[64:P, :], second[64:P, :], k.kk[64:P, :], ALU.mult)
                dve.drain()
                nc.vector.tensor_copy(second[64:P, :], first[64:P, :])
                dve.drain()
                nc.vector.tensor_copy(first[64:P, :], k.tmp[64:P, :])
                dve.drain()


def hold(pe, passed, sem, value):
    pe.wait_ge(sem, value)
    pe.sem_inc(passed, 1)


def rwkv_scan(nc, k, p):
    S = k.rsem
    past = lambda n: not (isinstance(n, int) and n == 0)
    q0 = 5 * p
    bank = [[k.psum[:, 4 * d + b, :] for b in range(4)] for d in range(2)]
    wide = [k.psum[:, 4 * d:4 * d + 2, :] for d in range(2)]
    late = [k.psum[:, 4 * d + 2:4 * d + 4, :] for d in range(2)]
    sides = lambda e: slice(64 * e, 64 * e + 64)

    def start_col(q, d):
        if isinstance(q, int):
            return 0 if q == 0 else (q * BT if d == 0 else (5 - q) * BT)
        return q * BT if d == 0 else (q * -BT) + 5 * BT

    def run(eng, body):
        body(0, False)
        with eng.Fori(1, 4) as q:
            body(q, False)
        body(4, True)

    with k.stage(nc) as block:
        @block.vector
        def _(dve):
            def stage(q):
                dve.drain()
                for d in range(2):
                    s, t = k.dir[d], S[d]
                    if past(q) or p:
                        dve.wait_ge(t["products"], q + q0)
                    cols = bass.ds(start_col(q, d), BT)
                    pd = k.pd[d]
                    v3 = lambda x: x[:, cols].rearrange("p (c n) -> p c n", c=NB)
                    nc.vector.tensor_tensor(s.qr[:, :, 0, :], v3(k.kk), v3(pd[1]), ALU.mult)
                    nc.vector.tensor_tensor(s.qr[:, :, 1, :], v3(k.r), v3(pd[0]), ALU.mult)
                    nc.vector.tensor_tensor(s.kb[:, :, 0, :], v3(pd[3]), v3(pd[2]), ALU.mult)
                    nc.vector.tensor_tensor(s.kb[:, :, 1, :], v3(pd[4]), v3(pd[2]), ALU.mult).then_inc(t["staged"], 1)

            def body(q, last):
                n = q + q0
                for d in range(2):
                    s, t = k.dir[d], S[d]
                    dve.wait_ge(t["products"], n + 1)
                    nc.vector.tensor_tensor(
                        s.kbs[:, :, :, :], late[d][:, :, 0:BT].rearrange("p e (c n) -> p c e n", c=NB),
                        k.sign[:, :, :].unsqueeze(1).to_broadcast([P, NB, 2, CH]), ALU.mult).then_inc(t["kb_kept"], 1)
                    nc.vector.tensor_tensor(
                        s.m1[:, :, :, :], wide[d].rearrange("p e (c n) -> p c e n", c=NB),
                        k.mask[d][:, :, :].unsqueeze(1).to_broadcast([P, NB, 2, P]), ALU.mult)
                    dve.drain()
                    for e in range(2):
                        u = sides(1 - e)
                        m = nc.vector.tensor_copy(s.a_t[u, :, :], s.m1[u, :, e, 0:CH])
                    m.then_inc(t["masked"], 1)
                for d in range(2):
                    s, t = k.dir[d], S[d]
                    eye = k.id64[:, :].unsqueeze(1).to_broadcast([P, NB, CH])
                    dve.wait_ge(t["levels"], n + 1)
                    nc.vector.tensor_tensor(s.tt[:, 1], eye, s.atl[:, 0], ALU.subtract)
                    dve.wait_ge(t["started"], n + 1)
                    nc.vector.tensor_tensor(s.tt[:, 0], eye, bank[d][0][:, 0:BT].rearrange("p (c n) -> p c n", c=NB),
                                            ALU.subtract).then_inc(t["t_ready"], 1)
                for level in range(5):
                    for d in range(2):
                        s, t = k.dir[d], S[d]
                        dve.wait_ge(t["update_done"], n * 5 + level + 1)
                        lo = 1 if level == 4 else 0
                        both = s.tt[:, lo:2].rearrange("p a c n -> p (a c n)")
                        nc.vector.tensor_tensor(both, both, bank[d][1][:, lo * BT:2 * BT],
                                                ALU.subtract).then_inc(t["updated"], 1)
                for d in range(2):
                    s, t = k.dir[d], S[d]
                    dve.wait_ge(t["g_done"], n + 1)
                    nc.vector.tensor_tensor(s.yg[:, 0], bank[d][3][:, 0:BT].rearrange("p (c n) -> p c n", c=NB),
                                            s.qr[:, :, 1, :], ALU.add)
                    nc.vector.tensor_tensor(s.yg[:, 1], bank[d][3][:, BT:2 * BT].rearrange("p (c n) -> p c n", c=NB),
                                            k.id64[:, :].unsqueeze(1).to_broadcast([P, NB, CH]),
                                            ALU.add).then_inc(t["g_kept"], 1)
                if not last:
                    stage(q + 1)
                for j in range(NB):
                    for d in range(2):
                        s, t = k.dir[d], S[d]
                        c = j if d == 0 else NB - 1 - j
                        end = c * CH + (CH - 1 if d == 0 else 0)
                        dve.wait_ge(t["h_done"], n * NB + j + 1)
                        nc.vector.tensor_scalar(s.h[:, (j + 1) % NB, :], bank[d][0][:, j * CH:(j + 1) * CH],
                                                k.pd[d][0][:, bass.ds(start_col(q, d) + end, 1)], None,
                                                ALU.mult).then_inc(t["h_kept"], 1)
            stage(0)
            for d in range(2):
                nc.vector.memset(k.dir[d].h[:, 0, :], 0.0)
                dve.drain().then_inc(S[d]["cleared"], 1)
            run(dve, body)

        @block.gpsimd
        def _(pool):
            def body(q, last):
                n = q + q0
                for d in range(2):
                    s, t = k.dir[d], S[d]
                    pool.wait_ge(t["masked"], n + 1)
                    nc.gpsimd.tensor_tensor(
                        s.atl[:, :, :, :], s.a_t[:, :, :].unsqueeze(1).to_broadcast([P, 6, NB, CH]),
                        k.maskl[d][:, :, :].unsqueeze(2).to_broadcast([P, 6, NB, CH]), ALU.mult).then_inc(t["levels"], 1)
            run(pool, body)

        @block.scalar
        def _(act):
            def stage(q):
                for d in range(2):
                    s, t = k.dir[d], S[d]
                    if past(q) or p:
                        act.wait_ge(t["products"], q + q0)
                    nc.scalar.activation(s.vs[:, :, :].rearrange("p c n -> p (c n)"),
                                         k.v[:, bass.ds(start_col(q, d), BT)], ACT.Copy).then_inc(t["v_staged"], 1)

            def body(q, last):
                n = q + q0
                for d in range(2):
                    s, t = k.dir[d], S[d]
                    act.wait_ge(t["kb_kept"], n + 1)
                    for e in range(2):
                        turned = bank[d][2 + e][:, BT:2 * BT].rearrange("p (c n) -> p c n", c=NB)
                        nc.scalar.activation(s.z[sides(1 - e), :, 0:CH], turned[sides(1 - e)], ACT.Copy)
                        m = nc.scalar.activation(s.vu[sides(e), :, e, :], turned[sides(e)], ACT.Copy)
                    m.then_inc(t["turned"], 1)
                for d in range(2):
                    s, t = k.dir[d], S[d]
                    act.wait_ge(t["started"], n + 1)
                    nc.scalar.activation(s.z[:, :, CH:P], bank[d][2][:, 0:BT].rearrange("p (c n) -> p c n", c=NB),
                                         ACT.Copy).then_inc(t["akv_kept"], 1)
                for level in range(5):
                    for d in range(2):
                        s, t = k.dir[d], S[d]
                        act.wait_ge(t["x_done"], n * 5 + level + 1)
                        nc.scalar.activation(s.x[:, :, :].rearrange("p c n -> p (c n)"), bank[d][0][:, 0:BT],
                                             ACT.Copy).then_inc(t["x_kept"], 1)
                for d in range(2):
                    s, t = k.dir[d], S[d]
                    w = bank[d][2].rearrange("p (c n) -> p c n", c=NB)
                    act.wait_ge(t["w_done"], n + 1)
                    nc.scalar.activation(s.w1[:, :, :], w[:, :, 0:CH], ACT.Copy)
                    for e in range(2):
                        m = nc.scalar.activation(s.vu[sides(1 - e), :, e, :], w[sides(1 - e), :, CH:P], ACT.Copy)
                    m.then_inc(t["w_kept"], 1)
                if not last:
                    stage(q + 1)
                if past(q):
                    for d in range(2):
                        t = S[d]
                        act.wait_ge(t["y_done"], n + 1)
                        nc.scalar.activation(k.yf[d][:, bass.ds(start_col(q, d) - CTX, BT)], bank[d][1][:, 0:BT],
                                             ACT.Copy).then_inc(t["y_kept"], 1)
                else:
                    for d in range(2):
                        act.wait_ge(S[d]["y_done"], n + 1)
                        nc.scalar.activation(k.tmp[:, BT * d:BT * d + BT], bank[d][1][:, 0:BT],
                                             ACT.Copy).then_inc(S[d]["y_kept"], 1)
            stage(0)
            run(act, body)

        @block.tensor
        def _(pe):
            mm = nc.tensor.matmul

            def body(q, last):
                n = q + q0
                for d in range(2):
                    s, t, b = k.dir[d], S[d], bank[d]
                    hold(pe, k.passed, t["staged"], n + 1)
                    hold(pe, k.passed, t["v_staged"], n + 1)
                    if past(q) or p:
                        hold(pe, k.passed, t["h_kept"], n * NB)
                        hold(pe, k.passed, t["y_kept"], n)
                        hold(pe, k.passed, t["w_kept"], n)
                        hold(pe, k.passed, t["g_kept"], n)
                    for c in range(NB):
                        for e in range(2):
                            v, u = sides(e), sides(1 - e)
                            kb = s.kb[v, c, :, :].rearrange("p a n -> p (a n)")
                            late_b = b[2 + e]
                            mm(b[e][:, c * P:(c + 1) * P], kb,
                               s.qr[v, c, :, :].rearrange("p a n -> p (a n)"), start=True, stop=True)
                            mm(late_b[:, c * CH:(c + 1) * CH], kb, k.id64[v, :], start=True, stop=True)
                            mm(late_b[u, BT + c * CH:BT + (c + 1) * CH], s.qr[v, c, 0, :], k.id64[v, :],
                               start=True, stop=True)
                            m = mm(late_b[v, BT + c * CH:BT + (c + 1) * CH], s.vs[v, c, :], k.id64[v, :],
                                   start=True, stop=True)
                    m.then_inc(t["products"], 1)
                for d in range(2):
                    s, t, b = k.dir[d], S[d], bank[d]
                    hold(pe, k.passed, t["masked"], n + 1)
                    hold(pe, k.passed, t["turned"], n + 1)
                    for c in range(NB):
                        for e in range(2):
                            v, u = sides(e), sides(1 - e)
                            mm(b[2][u, c * CH:(c + 1) * CH], s.m1[v, c, e, 0:CH], s.vu[v, c, e, :],
                               start=True, stop=True)
                    hold(pe, k.passed, t["levels"], n + 1)
                    for c in range(NB):
                        for h in range(2):
                            u = sides(h)
                            m = mm(b[0][u, c * CH:(c + 1) * CH], s.atl[u, 0, c, :], k.id64[u, :], start=True, stop=True)
                    m.then_inc(t["started"], 1)
                for level in range(5):
                    for d in range(2):
                        s, t, b = k.dir[d], S[d], bank[d]
                        if level == 0:
                            hold(pe, k.passed, t["t_ready"], n + 1)
                        else:
                            hold(pe, k.passed, t["updated"], n * 5 + level)
                        for c in range(NB):
                            for h in range(2):
                                u = sides(h)
                                m = mm(b[0][u, c * CH:(c + 1) * CH], s.atl[u, level + 1, c, :], s.tt[u, 0, c, :],
                                       start=True, stop=True)
                        m.then_inc(t["x_done"], 1)
                    for d in range(2):
                        s, t, b = k.dir[d], S[d], bank[d]
                        hold(pe, k.passed, t["x_kept"], n * 5 + level + 1)
                        for c in range(NB):
                            for h in range(2):
                                u = sides(h)
                                if level < 4:
                                    mm(b[1][u, c * CH:(c + 1) * CH], s.tt[u, 1, c, :], s.x[u, c, :],
                                       start=True, stop=True)
                                m = mm(b[1][u, BT + c * CH:BT + (c + 1) * CH], s.x[u, c, :], s.tt[u, 1, c, :],
                                       start=True, stop=True)
                        m.then_inc(t["update_done"], 1)
                for d in range(2):
                    s, t, b = k.dir[d], S[d], bank[d]
                    hold(pe, k.passed, t["updated"], n * 5 + 5)
                    hold(pe, k.passed, t["akv_kept"], n + 1)
                    for c in range(NB):
                        for h in range(2):
                            u = sides(h)
                            m = mm(b[2][u, c * P:(c + 1) * P], s.tt[u, 1, c, :], s.z[u, c, :], start=True, stop=True)
                    m.then_inc(t["w_done"], 1)
                for d in range(2):
                    s, t, b = k.dir[d], S[d], bank[d]
                    hold(pe, k.passed, t["w_kept"], n + 1)
                    for c in range(NB):
                        for e in range(2):
                            v, u = sides(e), sides(1 - e)
                            mm(b[3][v, c * CH:(c + 1) * CH], s.w1[u, c, :], s.m1[u, c, e, CH:P], start=True, stop=True)
                            m = mm(b[3][v, BT + c * CH:BT + (c + 1) * CH], s.w1[u, c, :], s.kbs[u, c, e, :],
                                   start=True, stop=True)
                    m.then_inc(t["g_done"], 1)
                for j in range(NB):
                    for d in range(2):
                        s, t, b = k.dir[d], S[d], bank[d]
                        c = j if d == 0 else NB - 1 - j
                        if j == 0:
                            hold(pe, k.passed, t["g_kept"], n + 1)
                            if not past(q):
                                pe.wait_ge(t["cleared"], p + 1)
                        else:
                            hold(pe, k.passed, t["h_kept"], n * NB + j)
                        for e in range(2):
                            v = sides(e)
                            mm(b[0][v, j * CH:(j + 1) * CH], s.kbs[:, c, e, :], s.vu[:, c, e, :], start=True, stop=False)
                            m = mm(b[0][v, j * CH:(j + 1) * CH], s.yg[v, 1, c, :], s.h[v, j, :], start=False, stop=True)
                        m.then_inc(t["h_done"], 1)
                        for e in range(2):
                            v = sides(e)
                            mm(b[1][v, c * CH:(c + 1) * CH], s.vu[:, c, e, :], s.m1[:, c, e, CH:P], start=True, stop=False)
                            m = mm(b[1][v, c * CH:(c + 1) * CH], s.h[v, j, :], s.yg[v, 0, c, :], start=False, stop=True)
                        if j == NB - 1:
                            m.then_inc(t["y_done"], 1)
            run(pe, body)


def rwkv_finish(nc, k, p):
    sem = k.sem
    names = ("summed", "mean", "centred", "squared", "var", "var_kept", "rooted", "bonus_in", "bonus", "gate")
    summed, mean, centred, squared, var, vark, rooted, bin_, bonus, gate = (sem(f"fin{p}_{n}") for n in names)
    ps = lambda b: k.psum[:, b:b + 2, :].rearrange("p a b -> p (a b)")
    y, yb = k.yf[0], k.yf[1]
    t1, t2 = k.pd[0][0], k.pd[1][0]
    main = slice(CTX, ALL)
    prm = lambda n: rows_of(k, n, p)
    with k.stage(nc) as block:
        @block.tensor
        def _(pe):
            def spread(b, lhs, rhs):
                for j in range(2):
                    last = nc.tensor.matmul(k.psum[:, b + j, :], lhs, rhs[:, j * 512:(j + 1) * 512], start=True, stop=True)
                return last
            spread(6, k.g2_w[:, p * P:(p + 1) * P], k.lora[:, 1, main]).then_inc(gate, 1)
            pe.wait_ge(summed, 1)
            spread(0, k.halves[:, :], y).then_inc(mean, 1)
            pe.wait_ge(bin_, 1)
            spread(4, k.halves[:, :], t2).then_inc(bonus, 1)
            pe.wait_ge(squared, 1)
            spread(2, k.halves[:, :], t1).then_inc(var, 1)

        @block.scalar
        def _(act):
            act.wait_ge(centred, 1)
            nc.scalar.activation(t1[:, 0:SEQ], yb[:, :], ACT.Square).then_inc(squared, 1)
            act.wait_ge(vark, 1)
            nc.scalar.activation(k.tmp[:, 0:SEQ], t1[:, 0:SEQ], ACT.Sqrt).then_inc(rooted, 1)

        @block.vector
        def _(dve):
            nc.vector.tensor_tensor(y[:, :], y[:, :], yb[:, :], ALU.add).then_inc(summed, 1)
            for e in range(2):
                h = slice(64 * e, 64 * e + 64)
                nc.vector.tensor_tensor(t2[h, 0:SEQ], k.pd[0][3 + e][h, main], k.pd[1][3 + e][h, main], ALU.add)
            dve.drain()
            nc.vector.tensor_tensor(t2[:, 0:SEQ], t2[:, 0:SEQ], k.r[:, main], ALU.mult)
            dve.drain()
            nc.vector.tensor_scalar(t2[:, 0:SEQ], t2[:, 0:SEQ], prm("r_k"), 0.5, ALU.mult, ALU.mult).then_inc(bin_, 1)
            dve.wait_ge(mean, 1)
            nc.vector.scalar_tensor_tensor(out=yb[:, :], in0=ps(0), scalar=-1.0 / CH, in1=y[:, :],
                                           op0=ALU.mult, op1=ALU.add).then_inc(centred, 1)
            dve.wait_ge(var, 1)
            nc.vector.tensor_scalar(t1[:, 0:SEQ], ps(2), 1.0 / CH, 64e-5, ALU.mult, ALU.add).then_inc(vark, 1)
            dve.wait_ge(bonus, 1)
            nc.vector.tensor_tensor(t2[:, 0:SEQ], ps(4), k.v[:, main], ALU.mult)
            dve.wait_ge(rooted, 1)
            nc.vector.reciprocal(k.tmp[:, 0:SEQ], k.tmp[:, 0:SEQ])
            dve.drain()
            nc.vector.tensor_tensor(yb[:, :], yb[:, :], k.tmp[:, 0:SEQ], ALU.mult)
            dve.drain()
            nc.vector.tensor_scalar(yb[:, :], yb[:, :], prm("ln_x_w"), prm("ln_x_b"), ALU.mult, ALU.add)
            dve.drain()
            nc.vector.tensor_tensor(yb[:, :], yb[:, :], t2[:, 0:SEQ], ALU.add)
            dve.drain()
            dve.wait_ge(gate, 1)
            nc.vector.tensor_tensor(k.ym[:, p, :], yb[:, :], ps(6), ALU.mult)


def rwkv(nc, k):
    rwkv_memory(nc, k)
    k.rsem = [{n: k.lasting(f"rw{d}_{n}") for n in STEPS + ("cleared",)} for d in range(2)]
    k.passed = k.lasting("rw_waits_passed")
    rwkv_setup(nc, k)
    for p in range(PAIRS):
        rwkv_prepare(nc, k, p)
        rwkv_scan(nc, k, p)
        rwkv_finish(nc, k, p)


def attention_memory(nc, k):
    o = [8192]

    def at(name, cols, dt=F32):
        t = k.at(name, cols, o[0], dt)
        o[0] += (4 * int(np.prod(cols)) + 31) // 32 * 32
        return t
    k.cos, k.sin = at("rope_cos", [SEQ]), at("rope_sin", [SEQ])
    k.qT, k.kT, k.vT = at("q_t", [SEQ]), at("k_t", [ALL]), at("v_t", [ALL])
    k.turn = at("half_turned", [SEQ])
    k.vtok = at("v_tokens", [KEYT, P])
    k.qs = [at(f"q_tile{s}", [P]) for s in range(2)]
    k.probs = [[at(f"probs{m}_{s}", [ALL]) for m in range(2)] for s in range(2)]
    k.mixT = [at(f"probs_t{s}", [KEYT, P]) for s in range(2)]
    k.mx = [at(f"max{s}", [2]) for s in range(2)]
    k.nmx = [at(f"neg_max{s}", [2]) for s in range(2)]
    k.sums = [at(f"sums{s}", [2]) for s in range(2)]
    k.inv = [at(f"inv{s}", [2]) for s in range(2)]
    k.oT = at("o_t", [SEQ])
    k.osq = at("o_sq", [SEQ])
    k.lamr = at("lam_rows", [4, 64])
    k.lamp = at("lam_products", [64])
    k.sub8 = at("subln_gain", [1])
    assert o[0] <= 180032, o[0]


def attention_setup(nc, k):
    sem = k.sem
    landed, dots, exps, lam1, spread = (sem(f"lam_{n}") for n in ("landed", "dots", "exps", "one", "spread"))
    ins = k.ins
    names = ("lam_q1", "lam_k1", "lam_q2", "lam_k2")
    with k.stage(nc) as block:
        @block.sync
        def _(sp):
            for j, n in enumerate(names):
                sp.dma_start(k.lamr[0:1, j, :], ins[n]).then_inc(landed, 16)
            sp.dma_start(k.cos[:, :], ins["cos_k"]).then_inc(landed, 16)
            sp.dma_start(k.sin[:, :], ins["sin_k"]).then_inc(landed, 16)
            sp.wait_ge(landed, 96)

        @block.vector
        def _(dve):
            dve.wait_ge(landed, 96)
            for j in range(2):
                nc.vector.tensor_tensor(k.lamp[0:1, :], k.lamr[0:1, 2 * j, :], k.lamr[0:1, 2 * j + 1, :], ALU.mult)
                dve.drain()
                nc.vector.tensor_reduce(k.lam[0:1, j:j + 1], k.lamp[0:1, :], AX.X, ALU.add)
                dve.drain()
            dve.drain().then_inc(dots, 1)
            dve.wait_ge(exps, 1)
            nc.vector.tensor_tensor(k.lam[0:1, 4:5], k.lam[0:1, 2:3], k.lam[0:1, 3:4], ALU.subtract)
            dve.drain()
            nc.vector.tensor_scalar(k.lam[0:1, 5:6], k.lam[0:1, 4:5], 0.8 - 0.6, None, ALU.add)
            dve.drain().then_inc(lam1, 1)
            dve.wait_ge(spread, 1)
            nc.vector.tensor_scalar(k.lam[:, 8:9], k.psum[:, 0, 0:1], -1.0, None, ALU.mult)
            nc.vector.tensor_scalar(k.sub8[:, :], rows_of(k, "subln_w"), 1.0 - (0.8 - 0.6), None, ALU.mult)

        @block.scalar
        def _(act):
            act.wait_ge(dots, 1)
            nc.scalar.activation(k.lam[0:1, 2:4], k.lam[0:1, 0:2], ACT.Exp).then_inc(exps, 1)

        @block.tensor
        def _(pe):
            pe.wait_ge(lam1, 1)
            nc.tensor.matmul(k.psum[:, 0, 0:1], k.ones[0:1, :], k.lam[0:1, 5:6], start=True, stop=True).then_inc(spread, 1)


def attention_head(nc, k, h):
    sem = k.sem
    pre = f"at{h}_"
    landed, turned, roped, vturned, vkept, scaled = (sem(pre + n) for n in
                                                     ("landed", "turned", "roped", "v_turned", "v_kept", "rotated"))
    q_staged, scores, maxed, negated, summed, mixed = (sem(pre + n) for n in
                                                       ("q_staged", "scores", "maxed", "negated", "summed", "mixed"))
    flipped, flip_kept, o_done, o_kept = (sem(pre + n) for n in ("flipped", "flip_kept", "o_done", "o_kept"))
    squared, meaned, eps_added, rooted = (sem(pre + n) for n in ("squared", "meaned", "eps_added", "rooted"))
    scale = 64.0 ** -0.5
    QT = SEQ // P
    past = lambda n, least: not (isinstance(n, int) and n < least)
    score = [k.psum[:, 3 * m:3 * m + 3, :].rearrange("p a b -> p (a b)")[:, 0:ALL] for m in range(2)]
    groups = ((0, 4, 6), (4, 8, 7), (8, 10, 6))
    out = k.psum[:, 7, 0:P]
    quarters = [slice(32 * j, 32 * j + 32) for j in range(4)]

    with k.stage(nc) as block:
        @block.sync
        def _(sp):
            for dst, n, cols in ((k.qT, h, slice(CTX, ALL)), (k.kT, 4 + h, slice(0, ALL)), (k.vT, 8 + h, slice(0, ALL))):
                sp.dma_start(dst[:, :], k.qkv_dram[n][:, cols]).then_inc(landed, 16)
            sp.wait_ge(landed, 48)

        @block.tensor
        def _(pe):
            pe.wait_ge(landed, 48)
            for j, (a, b, bank) in enumerate(((0, 4, 0), (4, 8, 1), (8, 10, 2))):
                for t in range(a, b):
                    last = nc.tensor.transpose(k.psum[:, bank, (t - a) * P:(t - a + 1) * P],
                                               k.vT[:, t * P:(t + 1) * P], k.ident[:, :])
                last.then_inc(vturned, 1)
            pe.wait_ge(vkept, 3)
            pe.wait_ge(roped, 1)

            def body(n, m, s):
                pe.wait_ge(q_staged, n + 1)
                if past(n, 1):
                    pe.wait_ge(summed, n)
                for mp in range(2):
                    r = slice(64 * mp, 64 * mp + 64)
                    for c, w in ((0, 512), (512, 512), (1024, 256)):
                        last = nc.tensor.matmul(score[mp][:, c:c + w], k.qs[s][r, :], k.kT[r, c:c + w],
                                                start=True, stop=True)
                last.then_inc(scores, 1)
                if past(n, 1):
                    values(n - 1, 1 - s)

            def values(n, s):
                pe.wait_ge(mixed, n + 1)
                for j, (a, b, bank) in enumerate(groups):
                    if j == 0:
                        if past(n, 1):
                            pe.wait_ge(flip_kept, n * 3)
                    elif j == 1:
                        if past(n, 1):
                            pe.wait_ge(o_kept, n)
                    else:
                        pe.wait_ge(flip_kept, n * 3 + 1)
                    for t in range(a, b):
                        last = nc.tensor.transpose(k.psum[:, bank, (t - a) * P:(t - a + 1) * P],
                                                   k.probs[s][0][:, t * P:(t + 1) * P], k.ident[:, :])
                    last.then_inc(flipped, 1)
                pe.wait_ge(flip_kept, n * 3 + 3)
                for t in range(KEYT):
                    last = nc.tensor.matmul(out, k.vtok[:, t, :], k.mixT[s][:, t, :],
                                            start=(t == 0), stop=(t == KEYT - 1))
                last.then_inc(o_done, 1)

            split_tiles(pe, QT, body)
            values(QT - 1, (QT - 1) % 2)
            pe.wait_ge(o_kept, QT)
            pe.wait_ge(squared, 1)
            for j in range(2):
                last = nc.tensor.matmul(k.psum[:, j, :], k.ones[:, :], k.osq[:, j * 512:(j + 1) * 512],
                                        start=True, stop=True)
            last.then_inc(meaned, 1)

        @block.scalar
        def _(act):
            act.wait_ge(landed, 48)
            for i, src in enumerate((k.qT[:, :], k.kT[:, CTX:ALL])):
                if i:
                    act.wait_ge(scaled, 1)
                for j in range(4):
                    last = nc.scalar.activation(k.turn[quarters[j ^ 1], :], src[quarters[j], :], ACT.Copy)
                last.then_inc(turned, 1)
            for j, (a, b, bank) in enumerate(((0, 4, 0), (4, 8, 1), (8, 10, 2))):
                act.wait_ge(vturned, j + 1)
                nc.scalar.activation(k.vtok[:, a:b, :].rearrange("p t n -> p (t n)"),
                                     k.psum[:, bank, 0:(b - a) * P], ACT.Copy).then_inc(vkept, 1)
            act.wait_ge(roped, 1)

            def stage(n, s):
                if past(n, 2):
                    act.wait_ge(scores, n - 1)
                nc.scalar.activation(k.qs[s][:, :], k.qT[:, bass.ds(n * P, P)], ACT.Copy).then_inc(q_staged, 1)

            def body(n, m, s):
                if not (isinstance(n, int) and n == QT - 1):
                    stage(n + 1, 1 - s)
                act.wait_ge(maxed, n + 1)
                nc.scalar.activation(k.nmx[s][:, :], k.mx[s][:, :], ACT.Copy, scale=-scale).then_inc(negated, 1)
                act.wait_ge(negated, n + 1)
                if past(n, 2):
                    act.wait_ge(flipped, n * 3 - 3)
                for mp in range(2):
                    last = nc.scalar.activation(k.probs[s][mp][:, :], score[mp], ACT.Exp,
                                                bias=k.nmx[s][:, mp:mp + 1], scale=scale,
                                                accum_out=k.sums[s][:, mp:mp + 1])
                act.drain().then_inc(summed, 1)
                if past(n, 1):
                    keep(n - 1, 1 - s)

            def keep(n, s):
                for j, (a, b, bank) in enumerate(groups):
                    act.wait_ge(flipped, n * 3 + j + 1)
                    nc.scalar.activation(k.mixT[s][:, a:b, :].rearrange("p t n -> p (t n)"),
                                         k.psum[:, bank, 0:(b - a) * P], ACT.Copy).then_inc(flip_kept, 1)
            stage(0, 0)
            split_tiles(act, QT, body)
            keep(QT - 1, (QT - 1) % 2)
            act.wait_ge(o_kept, QT)
            nc.scalar.activation(k.osq[:, :], k.oT[:, :], ACT.Square).then_inc(squared, 1)
            act.wait_ge(eps_added, 1)
            nc.scalar.activation(k.osq[:, :], k.osq[:, :], ACT.Sqrt).then_inc(rooted, 1)

        @block.vector
        def _(dve):
            for i, (dst, src) in enumerate(((k.qT, k.qT[:, :]), (k.kT, k.kT[:, CTX:ALL]))):
                dve.wait_ge(turned, i + 1)
                nc.vector.tensor_tensor(k.turn[:, :], k.turn[:, :], k.sin[:, :], ALU.mult)
                nc.vector.tensor_tensor(src, src, k.cos[:, :], ALU.mult)
                dve.drain()
                nc.vector.tensor_tensor(src, src, k.turn[:, :], ALU.add)
                dve.drain().then_inc(scaled, 1)
            dve.drain().then_inc(roped, 1)

            def body(n, m, s):
                dve.wait_ge(scores, n + 1)
                for mp in range(2):
                    last = nc.vector.tensor_reduce(k.mx[s][:, mp:mp + 1], score[mp], AX.X, ALU.max)
                last.then_inc(maxed, 1)
                if past(n, 1):
                    keep(n - 1, 1 - s)
                dve.wait_ge(summed, n + 1)
                nc.vector.reciprocal(k.inv[s][:, :], k.sums[s][:, :])
                dve.drain()
                nc.vector.tensor_tensor(k.inv[s][:, 1:2], k.inv[s][:, 1:2], k.lam[:, 8:9], ALU.mult)
                dve.drain()
                nc.vector.tensor_scalar(k.probs[s][1][:, :], k.probs[s][1][:, :], k.inv[s][:, 1:2], None, ALU.mult)
                dve.drain()
                nc.vector.scalar_tensor_tensor(out=k.probs[s][0][:, :], in0=k.probs[s][0][:, :],
                                               scalar=k.inv[s][:, 0:1], in1=k.probs[s][1][:, :],
                                               op0=ALU.mult, op1=ALU.add).then_inc(mixed, 1)

            def keep(n, s):
                dve.wait_ge(o_done, n + 1)
                nc.vector.tensor_copy(k.oT[:, bass.ds(n * P, P)], out).then_inc(o_kept, 1)
            split_tiles(dve, QT, body)
            keep(QT - 1, (QT - 1) % 2)
            dve.wait_ge(meaned, 1)
            nc.vector.tensor_scalar(k.osq[:, :], k.psum[:, 0:2, :].rearrange("p a b -> p (a b)"), 1.0 / P, 1e-5,
                                    ALU.mult, ALU.add).then_inc(eps_added, 1)
            dve.wait_ge(rooted, 1)
            nc.vector.reciprocal(k.osq[:, :], k.osq[:, :])
            dve.drain()
            nc.vector.scalar_tensor_tensor(out=k.ym[:, PAIRS + h, :], in0=k.oT[:, :], scalar=k.sub8[:, 0:1],
                                           in1=k.osq[:, :], op0=ALU.mult, op1=ALU.mult)


def attention(nc, k):
    attention_memory(nc, k)
    attention_setup(nc, k)
    for h in range(HEADS):
        attention_head(nc, k, h)


def split_resident(nc, k, name, src, hi, lo, tiles, n):
    high = k.sem(f"{name}_high")
    with k.stage(nc) as block:
        @block.scalar
        def _(act):
            for kk in range(tiles):
                nc.scalar.activation(hi[:, kk, 0:n], src[:, kk, 0:n], ACT.Copy).then_inc(high, 1)

        @block.vector
        def _(dve):
            for kk in range(tiles):
                dve.wait_ge(high, kk + 1)
                nc.vector.tensor_tensor(lo[:, kk, 0:n], src[:, kk, 0:n], hi[:, kk, 0:n].bitcast(F32), ALU.subtract)


def project_out(nc, k, name, w, hi, lo, pieces, out, n):
    wv = w.rearrange("(k p) n -> p k n", p=P)
    width = pieces[0][1]

    def evac(act, t, m, s, acc_read, worked):
        flat = out.rearrange("p k n -> p (k n)")
        dst = flat[:, bass.ds(t * out.shape[2], n)].rearrange("p (a b) -> p a b", b=width)
        nc.scalar.activation(dst, k.psum[:, 3 * s:3 * s + len(pieces), 0:width], ACT.Copy).then_inc(acc_read, 1)
    project(nc, k, name, KD, hi, lo, pieces, KD, lambda t: wv[:, :, bass.ds(t * P, P)], evac)


def load_resident(nc, k, name, dst, dram):
    landed = k.sem(f"{name}_landed")
    with k.stage(nc) as block:
        @block.sync
        def _(sp):
            sp.dma_start(dst, dram.rearrange("k p n -> p k n")).then_inc(landed, 16)
            sp.wait_ge(landed, 16)


def add_normed(nc, k, x, y, gain, n):
    with k.stage(nc) as block:
        @block.vector
        def _(dve):
            for kk in range(KD):
                nc.vector.tensor_tensor(k.sq[:, kk % 2, 0:n], y[:, kk, 0:n], k.rbc[:, 0:n], ALU.mult)
                dve.drain()
                nc.vector.scalar_tensor_tensor(out=x[:, kk, 0:n], in0=k.sq[:, kk % 2, 0:n], scalar=gain[:, kk:kk + 1],
                                               in1=x[:, kk, 0:n], op0=ALU.mult, op1=ALU.add)


def ffn_up(nc, k, name, w, conv, bias, active_first, func, pieces, data, left):
    wv = w.rearrange("(k p) n -> p k n", p=P)
    width, n_in = pieces[0][1], sum(c for _, c in pieces)
    offset = (0, KF) if active_first else (KF, 0)

    def weight(n):
        m, s = (n // 2, n % 2) if isinstance(n, int) else n
        return wv[:, :, bass.ds((m + offset[s]) * P, P)]

    def evac(act, n, m, s, acc_read, worked):
        nc.scalar.activation(k.xs[s][:, data:data + n_in].rearrange("p (a b) -> p a b", b=width),
                             k.psum[:, 3 * s:3 * s + len(pieces), 0:width], ACT.Copy).then_inc(acc_read, 1)
        if s == 1:
            act.wait_ge(worked, n)
            nc.scalar.activation(k.sg[:, :], k.ug[:, :], func).then_inc(activated, 1)

    def work(dve, n, m, s):
        u = k.uv if s else k.ug
        tap = [rows_of(k, f"{conv}{j}", m + offset[s]) for j in range(3)]
        x = k.xs[s]
        nc.vector.tensor_scalar(u[:, :], x[:, left + 1:left + 1 + SEQ], tap[1], rows_of(k, bias, m + offset[s]),
                                ALU.mult, ALU.add)
        for j in (0, 2):
            dve.drain()
            last = nc.vector.scalar_tensor_tensor(out=u[:, :], in0=x[:, left + j:left + j + SEQ], scalar=tap[j],
                                                  in1=u[:, :], op0=ALU.mult, op1=ALU.add)
        if s == 1:
            dve.drain()
            dve.wait_ge(activated, m + 1)
            last = nc.vector.tensor_tensor(tile_of(k.g, m), u[:, :], k.sg[:, :], ALU.mult)
        return last

    clear_pads(nc, k, (0, SEQ + 1) if data else (n_in,))
    activated = k.sem(f"{name}_activated")
    project(nc, k, name, KD, k.h_hi, k.h_lo, pieces, 2 * KF, weight, evac, work, pair_index=True)


def tile_of(t, m):
    return t[:, m, :] if isinstance(m, int) else t[:, bass.ds(m, 1), :].rearrange("p a n -> p (a n)")


def ffn_down(nc, k, name, w):
    wv = w.rearrange("(k p) n -> p k n", p=P)
    past = lambda n: not (isinstance(n, int) and n < 2)
    for half in range(2):
        sem = k.sem
        pre = f"{name}{half}_"
        landed = [sem(f"{pre}landed{s}") for s in range(2)]
        high, parts, used, total = (sem(pre + n) for n in ("high", "parts", "used", "total"))
        last_use = sem(pre + "complete")
        cols = 4 * P

        with k.stage(nc) as block:
            @block.sync
            def _(sp):
                def body(n, m, s):
                    if past(n):
                        sp.wait_ge(parts, n - 1)
                    sp.dma_start(k.w_raw[:, s, 0:cols],
                                 at_row_tile(wv, n, half * cols, cols)).then_inc(landed[s], 16)
                split_tiles(sp, KF, body)

            @block.scalar
            def _(act):
                def body(n, m, s):
                    act.wait_ge(landed[s], m * 16 + 16)
                    if past(n):
                        act.wait_ge(used, n - 1)
                    nc.scalar.activation(k.w_hi[:, s, 0:cols], k.w_raw[:, s, 0:cols], ACT.Copy)
                    nc.scalar.activation(k.g_hi[:, s, :], tile_of(k.g, n), ACT.Copy).then_inc(high, 1)
                split_tiles(act, KF, body)
                act.wait_ge(last_use, 1)
                for m in range(2):
                    nc.scalar.activation(k.y[:, 4 * half + m, :],
                                         k.psum[:, 2 * m:2 * m + 2, :].rearrange("p a b -> p (a b)"), ACT.Copy)

            @block.vector
            def _(dve):
                def body(n, m, s):
                    dve.wait_ge(high, n + 1)
                    nc.vector.tensor_tensor(k.w_lo[:, s, 0:cols], k.w_raw[:, s, 0:cols],
                                            k.w_hi[:, s, 0:cols].bitcast(F32), ALU.subtract)
                    nc.vector.tensor_tensor(k.g_lo[:, s, :], tile_of(k.g, n), k.g_hi[:, s, :].bitcast(F32),
                                            ALU.subtract).then_inc(parts, 1)
                split_tiles(dve, KF, body)
                dve.wait_ge(last_use, 1)
                for m in range(2, 4):
                    nc.vector.tensor_copy(k.y[:, 4 * half + m, :],
                                          k.psum[:, 2 * m:2 * m + 2, :].rearrange("p a b -> p (a b)"))

            @block.tensor
            def _(pe):
                def body(n, m, s):
                    first, end = isinstance(n, int) and n == 0, isinstance(n, int) and n == KF - 1
                    pe.wait_ge(parts, n + 1)
                    for c in range(4):
                        for q, (wp, gp) in enumerate(((k.w_hi, k.g_hi), (k.w_lo, k.g_hi), (k.w_hi, k.g_lo))):
                            for j in range(2):
                                last = nc.tensor.matmul(k.psum[:, 2 * c + j, :], wp[:, s, c * P:(c + 1) * P],
                                                        gp[:, s, j * 512:(j + 1) * 512],
                                                        start=(first and q == 0), stop=(end and q == 2))
                    last.then_inc(last_use if end else used, 1)
                split_tiles(pe, KF, body)


def at_row_tile(wv, n, c0, cols):
    return wv[:, n, c0:c0 + cols] if isinstance(n, int) else \
        wv[:, bass.ds(n, 1), c0:c0 + cols].rearrange("p a n -> p (a n)")


PIECES1 = [(0, 512), (512, 512)]
PIECES2 = [(j * PIECE2, PIECE2) for j in range(3)]
PIECES_FF2 = [(j * (FF2_IN // 3), FF2_IN // 3) for j in range(3)]


def finish_first(nc, k):
    ins = k.ins
    adaln_stage(nc, k, "mod2", 16, 48)
    a_hi = k.at("mix_hi", [KD, SEQ], 104576, F32R)
    a_lo = k.at("mix_lo", [KD, SEQ], 137344, F32R)
    split_resident(nc, k, "mix", k.ym, a_hi, a_lo, KD, SEQ)
    y = k.at("mix_y", [KD, SEQ], k.BIG)
    project_out(nc, k, "w_out", ins["w_out"][0], a_hi, a_lo, PIECES1, y, SEQ)
    x = k.at("x1", [KD, SEQ], 96384)
    load_resident(nc, k, "x1", x[:, :, :], k.x_dram)
    token_scale(nc, k, "post1", lambda kk: y[:, kk, :], SEQ, 1e-6)
    col = lambda n: k.prm[:, k.col[n]:k.col[n] + KD]
    gains(nc, k, "g2", [(k.scale[:, 2, :], col("g_post_mix"), k.mod[:, 16:24, 0], False),
                        (k.scale[:, 3, :], col("g_pre_ffn"), k.mod[:, 32:40, 0], True),
                        (k.scale[:, 4, :], col("g_post_ffn"), k.mod[:, 40:48, 0], False)])
    add_normed(nc, k, x, y, k.scale[:, 2, :], SEQ)
    save(nc, k, "x1_save", k.x_dram, x[:, :, :])
    token_scale(nc, k, "pre2", lambda kk: x[:, kk, :], SEQ, 1e-6)
    ffn_memory(nc, k)
    whole = slice(0, SEQ)
    modulate_split(nc, k, "h2", [(kk, x[:, kk, :], whole, whole, k.scale[:, 3, kk:kk + 1], k.mod[:, 24 + kk, 0:1])
                                 for kk in range(KD)], k.h_hi, k.h_lo)
    ffn_up(nc, k, "up1", ins["w_up"][0], "ffn_conv", "ffn_conv_b", False, ACT.Silu, PIECES1, 1, 0)
    ffn_down(nc, k, "down1", ins["w_down"][0])
    k.x2 = k.at("x2", [KD, PAD2], k.BIG)
    load_resident(nc, k, "x2", k.x2[:, :, META:L2], k.x_dram)
    token_scale(nc, k, "post2", lambda kk: k.y[:, kk, :], SEQ, 1e-6)
    add_normed(nc, k, k.x2[:, :, META:L2], k.y, k.scale[:, 4, :], SEQ)


def ffn_memory(nc, k):
    k.h_hi = k.at("h_hi_ffn", [KD, FF2_IN], k.SPLIT, F32R)
    k.h_lo = k.at("h_lo_ffn", [KD, FF2_IN], k.SPLIT + 4 * KD * FF2_IN, F32R)
    k.g = k.at("g", [KF, SEQ], 43136)
    k.g_hi = k.at("g_hi", [2, SEQ], k.SPLIT, F32R)
    k.g_lo = k.at("g_lo", [2, SEQ], k.SPLIT + 8192, F32R)
    k.y = k.at("y_ffn", [KD, SEQ], k.SPLIT + 16384)
    k.ug, k.uv, k.sg = (k.at(n, [SEQ], 198912 + 4096 * j) for j, n in enumerate(("u_gate", "u_val", "gated")))


def second_block(nc, k):
    ins = k.ins
    load_turned(nc, k, "meta", [(ins["meta_tokens_2"], META, 0)], k.x2)
    with k.stage(nc) as block:
        @block.vector
        def _(dve):
            nc.vector.memset(k.x2[:, :, L2:PAD2], 0.0)
            nc.vector.memset(k.rbc[:, L2:PAD2], 0.0)
    save(nc, k, "x2_save", k.x2_dram, k.x2[:, :, :])
    token_scale(nc, k, "pre3", lambda kk: k.x2[:, kk, 0:L2], L2, 1e-6)
    k.h_hi = k.at("h3_hi", [KD, PAD2], 105216, F32R)
    k.h_lo = k.at("h3_lo", [KD, PAD2], 105216 + 4 * KD * PAD2, F32R)
    whole = slice(0, PAD2)
    gain = lambda n, kk: rows_of(k, n, kk)
    modulate_split(nc, k, "h3", [(kk, k.x2[:, kk, :], whole, whole, gain("g_mix_pre_2", kk), 0.0)
                                 for kk in range(KD)], k.h_hi, k.h_lo)
    gated_conv(nc, k)
    fourier(nc, k)
    merge(nc, k)
    m = k.at("merged", [KD, PAD2], k.BIG)
    load_resident(nc, k, "merged", m[:, :, :], k.m_dram)
    a_hi = k.at("merged_hi", [KD, PAD2], 105216, F32R)
    a_lo = k.at("merged_lo", [KD, PAD2], 105216 + 4 * KD * PAD2, F32R)
    split_resident(nc, k, "merged", m, a_hi, a_lo, KD, PAD2)
    y = k.at("mix_y2", [KD, PAD2], k.BIG)
    project_out(nc, k, "w_out2", ins["w_out_2"][0], a_hi, a_lo, PIECES2, y, PAD2)
    x = k.at("x3", [KD, PAD2], 97024)
    load_resident(nc, k, "x3", x[:, :, :], k.x2_dram)
    token_scale(nc, k, "post3", lambda kk: y[:, kk, 0:L2], L2, 1e-6)
    add_normed(nc, k, x, y, k.prm[:, k.col["g_mix_post_2"]:k.col["g_mix_post_2"] + KD], L2)
    save(nc, k, "x3_save", k.x2_dram, x[:, :, :])
    token_scale(nc, k, "pre4", lambda kk: x[:, kk, 0:L2], L2, 1e-6)
    k.h_hi = k.at("h4_hi", [KD, FF2_IN], k.SPLIT, F32R)
    k.h_lo = k.at("h4_lo", [KD, FF2_IN], k.SPLIT + 4 * KD * FF2_IN, F32R)
    kept = slice(META - 2, L2)
    modulate_split(nc, k, "h4", [(kk, x[:, kk, kept], kept, slice(0, FF2_IN), gain("g_ffn_pre_2", kk), 0.0)
                                 for kk in range(KD)], k.h_hi, k.h_lo)
    ffn_up(nc, k, "up2", ins["w_up_2"][0], "conv_w_ffn_2", "conv_b_ffn_2", True, ACT.Gelu_apprx_tanh,
           PIECES_FF2, 0, 1)
    ffn_down(nc, k, "down2", ins["w_down_2"][0])
    x = k.at("x4", [KD, SEQ], k.BIG)
    load_resident(nc, k, "x4", x[:, :, :], k.x2_dram[:, :, META:L2])
    token_scale(nc, k, "post4", lambda kk: k.y[:, kk, :], SEQ, 1e-6)
    add_normed(nc, k, x, k.y, k.prm[:, k.col["g_ffn_post_2"]:k.col["g_ffn_post_2"] + KD], SEQ)
    write_turned(nc, k, x)


def gated_conv(nc, k):
    w = k.ins["w_in_2"][0].rearrange("(k p) n -> p k n", p=P)
    FW = 512
    cb = k.at("conv_branch", [4, PAD2], 79232)
    prod = k.at("c_times_v", [PAD2 + 2], 95936)
    tmp = k.at("gated_tmp", [PAD2], 100160)
    k.cb_hi = k.at("cb_hi", [4, PAD2], 172032, F32R)
    k.cb_lo = k.at("cb_lo", [4, PAD2], 172032 + 16 * PAD2, F32R)

    def evac(act, n, m, s, acc_read, worked):
        nc.scalar.activation(k.xs[s][:, 0:PAD2].rearrange("p (a b) -> p a b", b=PIECE2),
                             k.psum[:, 3 * s:3 * s + 3, 0:PIECE2], ACT.Copy).then_inc(acc_read, 1)

    def cv_work(dve, n, m, s):
        body = prod[:, 1:1 + L2]
        if s == 0:
            return nc.vector.tensor_copy(body, k.xs[0][:, 0:L2])
        nc.vector.tensor_tensor(body, body, k.xs[1][:, 0:L2], ALU.mult)
        dve.drain()
        tap = [rows_of(k, f"conv_w_mix_2{j}", m) for j in range(3)]
        out = tile_of(cb, m)[:, 0:L2]
        nc.vector.tensor_scalar(out, body, tap[1], rows_of(k, "conv_b_mix_2", m), ALU.mult, ALU.add)
        for j in (0, 2):
            dve.drain()
            last = nc.vector.scalar_tensor_tensor(out=out, in0=prod[:, j:j + L2], scalar=tap[j], in1=out,
                                                  op0=ALU.mult, op1=ALU.add)
        return last

    with k.stage(nc) as block:
        @block.vector
        def _(dve):
            nc.vector.memset(prod[:, 0:1], 0.0)
            nc.vector.memset(prod[:, 1 + L2:2 + L2], 0.0)
            nc.vector.memset(cb[:, :, L2:PAD2], 0.0)

    offset = (FW, 3 * FW)

    def cv_weight(n):
        m, s = (n // 2, n % 2) if isinstance(n, int) else n
        return w[:, :, bass.ds(m * P + offset[s], P)]
    project(nc, k, "cv", KD, k.h_hi, k.h_lo, PIECES2, 8, cv_weight, evac, cv_work, pair_index=True)

    def b_work(dve, n, m, s):
        nc.vector.tensor_tensor(tmp[:, :], tile_of(cb, n), k.xs[s][:, 0:PAD2], ALU.mult)
        dve.drain()
        nc.vector.tensor_copy(tile_of(k.cb_hi, n), tmp[:, :])
        dve.drain()
        return nc.vector.tensor_tensor(tile_of(k.cb_lo, n), tmp[:, :], tile_of(k.cb_hi, n).bitcast(F32), ALU.subtract)
    project(nc, k, "b_gate", KD, k.h_hi, k.h_lo, PIECES2, 4, lambda n: w[:, :, bass.ds(n * P + 2 * FW, P)],
            evac, b_work)

    k.u = k.at("fourier_in", [4, PAD2], 79232)

    def u_evac(act, n, m, s, acc_read, worked):
        nc.scalar.activation(tile_of(k.u, n).rearrange("p (a b) -> p a b", b=PIECE2),
                             k.psum[:, 3 * s:3 * s + 3, 0:PIECE2], ACT.Copy).then_inc(acc_read, 1)
    project(nc, k, "u_in", KD, k.h_hi, k.h_lo, PIECES2, 4, lambda n: w[:, :, bass.ds(n * P, P)], u_evac)


NT2 = (L2 + P - 1) // P
HALF = L2 // 2 + 1
CUT = (HALF + 1) // 2


def fourier(nc, k):
    cosl = k.at("dft_cos", [NT2, HALF], 8192)
    sinl = k.at("dft_sin", [NT2, HALF], 8192 + (4 * NT2 * HALF + 31) // 32 * 32)
    ab = k.at("channel_dft", [NT2, 2, P], 95936)
    f = k.at("fourier_out", [PAD2], 205440)
    even = k.at("even_part", [HALF + 3], 209632)
    chan = k.at("dft_channels", [2, P], 211744)
    k.f_hi = k.at("f_hi", [4, PAD2], 45824, F32R)
    k.f_lo = k.at("f_lo", [4, PAD2], 45824 + 16 * PAD2, F32R)
    size = [min(P, L2 - t * P) for t in range(NT2)]
    sem = k.sem
    landed, chans, chans_kept, evens, even_kept, f_done, f_high, f_low = (
        sem(f"dft_{n}") for n in ("landed", "channels", "channels_kept", "positions", "even_kept", "combined",
                                  "high", "low"))
    with k.stage(nc) as block:
        @block.sync
        def _(sp):
            full = (NT2 - 1) * P
            loads = [(chan[:, :, :], k.ins["dft_channels_k"])]
            for dst, name in ((cosl, "dft_cos_k"), (sinl, "dft_sin_k")):
                loads.append((dst[:, 0:NT2 - 1, :], k.ins[name][0:full].rearrange("(t p) n -> p t n", p=P)))
                loads.append((dst[0:size[-1], NT2 - 1, :], k.ins[name][full:L2]))
            for dst, src in loads:
                sp.dma_start(dst, src).then_inc(landed, 16)
            sp.wait_ge(landed, 16 * 5)

        @block.tensor
        def _(pe):
            pe.wait_ge(landed, 16 * 5)
            for g in range(4):
                if g:
                    pe.wait_ge(chans_kept, g * NT2)
                for t in range(NT2):
                    if t == NT2 - 1:
                        pe.wait_ge(chans_kept, g * NT2 + 2)
                    o = (t % 2) * 2 * P
                    nc.tensor.matmul(k.psum[0:size[t], (t // 2) % 4, o:o + 2 * P], k.u[:, g, t * P:t * P + size[t]],
                                     chan[:, :, :].rearrange("p a n -> p (a n)"), start=True, stop=True).then_inc(chans, 1)
                pe.wait_ge(chans_kept, (g + 1) * NT2)
                if g:
                    pe.wait_ge(f_done, g)
                for part, table in enumerate((cosl, sinl)):
                    for j, (c0, c1) in enumerate(((0, CUT), (CUT, HALF))):
                        for t in range(NT2):
                            last = nc.tensor.matmul(k.psum[:, 4 + 2 * part + j, 0:c1 - c0], ab[0:size[t], t, part, :],
                                                    table[0:size[t], t, c0:c1], start=(t == 0), stop=(t == NT2 - 1))
                last.then_inc(evens, 1)

        @block.scalar
        def _(act):
            for g in range(4):
                if g:
                    act.wait_ge(evens, g)
                for t in range(NT2):
                    act.wait_ge(chans, g * NT2 + (t + 1 if t == NT2 - 1 else 2 * (t // 2) + 2))
                    o = (t % 2) * 2 * P
                    nc.scalar.activation(ab[0:size[t], t, :, :].rearrange("p a n -> p (a n)"),
                                         k.psum[0:size[t], (t // 2) % 4, o:o + 2 * P], ACT.Copy).then_inc(chans_kept, 1)
                act.wait_ge(evens, g + 1)
                if g:
                    act.wait_ge(f_done, g)
                nc.scalar.activation(even[:, 0:CUT], k.psum[:, 4, 0:CUT], ACT.Copy)
                nc.scalar.activation(even[:, CUT:HALF], k.psum[:, 5, 0:HALF - CUT], ACT.Copy).then_inc(even_kept, 1)
                act.wait_ge(f_done, g + 1)
                nc.scalar.activation(k.f_hi[:, g, :], f[:, :], ACT.Copy).then_inc(f_high, 1)

        @block.vector
        def _(dve):
            nc.vector.memset(f[:, L2:PAD2], 0.0)
            for g in range(4):
                dve.wait_ge(even_kept, g + 1)
                dve.drain()
                nc.vector.tensor_tensor(f[:, 0:CUT], even[:, 0:CUT], k.psum[:, 6, 0:CUT], ALU.subtract)
                nc.vector.tensor_tensor(f[:, CUT:HALF], even[:, CUT:HALF], k.psum[:, 7, 0:HALF - CUT], ALU.subtract)
                nc.vector.tensor_tensor(f[:, L2 - 1:L2 - CUT:-1], even[:, 1:CUT], k.psum[:, 6, 1:CUT], ALU.add)
                nc.vector.tensor_tensor(f[:, L2 - CUT:HALF - 1:-1], even[:, CUT:HALF - 1],
                                        k.psum[:, 7, 0:HALF - 1 - CUT], ALU.add)
                dve.drain().then_inc(f_done, 1)
                dve.wait_ge(f_high, g + 1)
                nc.vector.tensor_tensor(k.f_lo[:, g, :], f[:, :], k.f_hi[:, g, :].bitcast(F32), ALU.subtract)


def merge(nc, k):
    w_in = k.ins["w_in_2"][0].rearrange("(k p) n -> p k n", p=P)
    wf = k.ins["w_fourier_2"][0].rearrange("(k p) n -> p k n", p=P)
    wc = k.ins["w_conv_out_2"][0].rearrange("(k p) n -> p k n", p=P)
    sig = [k.at(f"gate{s}", [PAD2], 79232 + 4192 * s) for s in range(2)]
    out = k.at("merged_tile", [PAD2], 79232 + 8384)
    tmp = k.at("merged_tmp", [PAD2], 79232 + 12576)
    mark = k.at("gate_mark", [1], 79232 + 12576 + (4 * PAD2 + 31) // 32 * 32)
    g0 = 4 * 512

    def weight(n):
        i, r = (n // 4, n % 4) if isinstance(n, int) else n
        if r < 2:
            return w_in[:, :, bass.ds(i * P + g0 + r * D, P)]
        return (wf if r == 2 else wc)[:, :, bass.ds(i * P, P)]

    def evac(act, n, i, r, acc_read, worked):
        s = r % 2
        src = k.psum[:, 3 * s:3 * s + 3, 0:PIECE2]
        v = lambda t: t[:, 0:PAD2].rearrange("p (a b) -> p a b", b=PIECE2)
        if r < 2:
            nc.scalar.activation(v(sig[r]), src, ACT.Sigmoid, bias=rows_of(k, "b_gates_2", i + KD * r)).then_inc(acc_read, 1)
        else:
            nc.scalar.activation(v(k.xs[s]), src, ACT.Copy).then_inc(acc_read, 1)

    def work(dve, n, i, r):
        if r < 2:
            return nc.vector.memset(mark[:, :], 0.0)
        if r == 2:
            return nc.vector.tensor_tensor(out[:, :], k.xs[0][:, 0:PAD2], sig[0][:, :], ALU.mult)
        nc.vector.tensor_tensor(tmp[:, :], k.xs[1][:, 0:PAD2], sig[1][:, :], ALU.mult)
        dve.drain()
        return nc.vector.tensor_tensor(out[:, :], out[:, :], tmp[:, :], ALU.add)

    acts = [(KD, k.h_hi, k.h_lo)] * 2 + [(4, k.f_hi, k.f_lo), (4, k.cb_hi, k.cb_lo)]
    project(nc, k, "merge", None, None, None, PIECES2, 4 * KD, weight, evac, work, quads=acts,
            store=lambda sp, i: sp.dma_start(at_tile(k.m_dram, i), out[:, :]))


def write_turned(nc, k, x):
    sem = k.sem
    turned = sem("out_turned")
    kept = [sem("out_kept_by_vector"), sem("out_kept_by_scalar")]
    stored = [sem(f"out_stored{s}") for s in range(2)]
    rows = [k.at(f"out_rows{s}", [D], k.SPLIT + 4096 * s) for s in range(2)]
    NT = SEQ // P
    with k.stage(nc) as block:
        @block.tensor
        def _(pe):
            for t in range(NT):
                if t >= 2:
                    for half in kept:
                        pe.wait_ge(half, t - 1)
                for kk in range(KD):
                    last = nc.tensor.transpose(k.psum[:, 2 * (t % 2) + kk // 4, (kk % 4) * P:(kk % 4 + 1) * P],
                                               x[:, kk, t * P:(t + 1) * P], k.ident[:, :])
                last.then_inc(turned, 1)

        @block.vector
        def _(dve):
            for t in range(NT):
                dve.wait_ge(turned, t + 1)
                if t >= 2:
                    dve.wait_ge(stored[t % 2], 16 * (t // 2))
                nc.vector.tensor_copy(rows[t % 2][:, 0:512], k.psum[:, 2 * (t % 2), :]).then_inc(kept[0], 1)

        @block.scalar
        def _(act):
            for t in range(NT):
                act.wait_ge(turned, t + 1)
                if t >= 2:
                    act.wait_ge(stored[t % 2], 16 * (t // 2))
                nc.scalar.activation(rows[t % 2][:, 512:D], k.psum[:, 2 * (t % 2) + 1, :], ACT.Copy).then_inc(kept[1], 1)

        @block.sync
        def _(sp):
            for t in range(NT):
                for half in kept:
                    sp.wait_ge(half, t + 1)
                sp.dma_start(k.out[0, t * P:(t + 1) * P, :], rows[t % 2][:, :]).then_inc(stored[t % 2], 16)
            for s in range(2):
                sp.wait_ge(stored[s], 16 * (NT // 2))


def program(nc, ins, out):
    k = Kit()
    k.ins = ins
    with ExitStack() as ctx:
        k.nc, k.taken = nc, []
        k.lasting = lambda n: ctx.enter_context(nc.semaphore(n))
        k.placed, k.col, k.n_batches = plan_params(ins)
        memory(nc, k)
        k.psum = ctx.enter_context(nc.psum_tensor("psum", [P, 8, 512], F32))
        kind = "Internal"
        k.rw_dram = nc.dram_tensor("rw_scratch", [14, P, ALL], F32, kind=kind).ap()
        k.qkv_dram = nc.dram_tensor("qkv_scratch", [12, P, ALL], F32, kind=kind).ap()
        k.out = out
        k.x2_dram = nc.dram_tensor("x2_scratch", [KD, P, PAD2], F32, kind="Internal").ap()
        k.m_dram = nc.dram_tensor("merged_scratch", [KD, P, PAD2], F32, kind="Internal").ap()
        k.y_dram = nc.dram_tensor("y_scratch", [KD, P, SEQ], F32, kind=kind).ap()
        k.x_dram = nc.dram_tensor("x_scratch", [KD, P, SEQ], F32, kind=kind).ap()
        first_block(nc, k)
        rwkv(nc, k)
        attention(nc, k)
        finish_first(nc, k)
        second_block(nc, k)


_INS = [
    "x", "c", "ctx", "c_ctx", "w_mod", "b_mod", "g_pre_mix", "g_post_mix", "g_pre_ffn", "g_post_ffn", "w_in",
    "rwkv_conv", "w0_fwd", "w2_fwd", "a0_fwd", "a2_fwd", "w0_bwd", "w2_bwd", "a0_bwd", "a2_bwd", "g2", "k_k",
    "k_a", "r_k", "ln_x_w", "ln_x_b", "lam_q1", "lam_k1", "lam_q2", "lam_k2", "subln_w", "w_out", "w_up",
    "ffn_conv", "ffn_conv_b", "w_down", "meta_tokens_2", "g_mix_pre_2", "w_in_2", "b_gates_2", "w_fourier_2",
    "conv_w_mix_2", "conv_b_mix_2", "w_conv_out_2", "w_out_2", "g_mix_post_2", "g_ffn_pre_2", "w_up_2",
    "conv_w_ffn_2", "conv_b_ffn_2", "w_down_2", "g_ffn_post_2"]


def tables():
    t = {}
    half = np.kron(np.eye(2), np.ones((CH, CH)))
    t["halves_k"] = half
    strict = np.triu(np.ones((CH, CH)), 1)
    incl = np.triu(np.ones((CH, CH)))
    masks, levels = [], []
    for d in range(2):
        turn = (lambda a: a) if d == 0 else (lambda a: a[::-1, ::-1])
        vals = np.concatenate([turn(strict), turn(incl)], 1)
        us = np.concatenate([turn(strict), -turn(incl)], 1)
        masks.append(np.stack([np.concatenate([vals, us], 0), np.concatenate([us, vals], 0)], 1))
        i = np.arange(CH)
        lev = [strict * ((i[:, None] >> (b + 1)) == (i[None] >> (b + 1))) * ((i[:, None] >> b) != (i[None] >> b))
               for b in range(6)]
        levels.append(np.tile(np.stack([turn(m) for m in lev], 1), (2, 1, 1)))
    t["mask_k"] = np.stack(masks)
    t["levels_k"] = np.stack(levels)
    sign = np.ones((P, 2, CH))
    sign[CH:, 0] = -1
    sign[:CH, 1] = -1
    t["sign_k"] = sign
    rows, n_pair = SEQ // GRID_W, 16
    inv = 10000.0 ** (-np.arange(n_pair, dtype=np.float32) / np.float32(n_pair))
    row = np.repeat(np.arange(rows, dtype=np.float32), GRID_W)
    colm = np.tile(np.arange(GRID_W, dtype=np.float32), rows)
    ang = np.concatenate([row[:, None] * inv, colm[:, None] * inv], 1).astype(np.float32).astype(np.float64).T
    t["cos_k"] = np.tile(np.cos(ang), (4, 1))
    t["sin_k"] = np.tile(np.concatenate([-np.sin(ang), np.sin(ang)], 0), (2, 1))
    l = np.arange(L2)[:, None] * np.arange(L2 // 2 + 1)[None] % L2
    t["dft_cos_k"] = np.cos(2 * np.pi * l / L2)
    t["dft_sin_k"] = np.sin(2 * np.pi * l / L2)
    c = 2 * np.pi * (np.arange(P)[:, None] * np.arange(P)[None] % P) / P
    t["dft_channels_k"] = np.stack([np.cos(c), np.sin(c)], 1) / np.sqrt(L2 * P)
    t["id64_k"] = np.tile(np.eye(CH), (2, 1))
    return {n: np.ascontiguousarray(a, dtype=np.float32) for n, a in t.items()}


def kernel(**inputs):
    import concourse.bacc as bacc
    from concourse.bass_utils import run_bass_kernel_spmd

    nc = bacc.Bacc("TRN2", target_bir_lowering=False, num_devices=1)
    arrays, ins = {}, {}
    for name, a in [(n, inputs[n]) for n in _INS] + list(tables().items()):
        a = np.ascontiguousarray(a)
        arrays[f"in_{name}"] = a
        ins[name] = nc.dram_tensor(f"in_{name}", a.shape, mybir.dt.from_np(a.dtype), kind="ExternalInput").ap()
    out = nc.dram_tensor("out", (1, SEQ, D), F32, kind="ExternalOutput").ap()
    program(nc, ins, out)
    got = run_bass_kernel_spmd(nc, [arrays], core_ids=[0])
    return got.results[0]["out"]
```
